# Optimizing a Trainium2 kernel written in Bass

```python
import math
import jax, jax.numpy as jnp
from jax import lax
import numpy as np
import jax
import jax.numpy as jnp

D_MODEL = 1024
BATCH = 1
SEQ = 256
DEPTH = 2

M_HEADS = 4
M_HEAD_DIM = 256
M_WIDTH = M_HEADS * M_HEAD_DIM
M_CHUNK = 128
CONV_WIDTH = 5
ATT_SLOTS = 8
ATT_HEAD_DIM = 64
ATT_PATTERNS = ((128, 1), (512, 4), (2048, 16))
N_PATTERNS = 3
ATT_HEADS = ATT_SLOTS * N_PATTERNS
ATT_WIDTH = ATT_HEADS * ATT_HEAD_DIM
ATT_OUT = ATT_SLOTS * ATT_HEAD_DIM
D_FF = -(-8 * D_MODEL // (3 * 256)) * 256
DN_ALPHA = (2 * DEPTH) ** 0.25
DN_BETA = (8 * DEPTH) ** -0.25
LN_EPS = 1e-5
NEG = -1e30
IN_SECTIONS = (2 * M_WIDTH, M_WIDTH, M_WIDTH, 4 * M_HEADS, 3 * ATT_WIDTH, 2 * D_MODEL)
N_IN = sum(IN_SECTIONS)


def layer_norm(x, g=None, b=None):
    xf = x.astype(jnp.float32)
    mu = xf.mean(-1, keepdims=True)
    var = jnp.square(xf - mu).mean(-1, keepdims=True)
    y = (xf - mu) * lax.rsqrt(var + LN_EPS)
    if g is not None:
        y = y * g.astype(jnp.float32) + b.astype(jnp.float32)
    return y.astype(x.dtype)

def alibi_slopes():
    h = np.arange(1, ATT_HEADS + 1, dtype=np.float32)
    s = np.exp2(-8.0 * h / ATT_HEADS).astype(np.float32)
    return jnp.asarray(s.reshape(N_PATTERNS, ATT_SLOTS))

def centred_dwconv(x, w, b):
    k, ch = w.shape
    y = lax.conv_general_dilated(x, w[:, None, :], window_strides=(1,),
                                 padding=((k // 2, k // 2),),
                                 dimension_numbers=('NWC', 'WIO', 'NWC'),
                                 feature_group_count=ch)
    return y + b

def mlstm_scan(q, k, v, i_pre, f_pre):
    B, H, S, dk = q.shape
    dv = v.shape[-1]
    nc = S // M_CHUNK

    def chunks(a):
        return jnp.moveaxis(a.reshape(B, H, nc, M_CHUNK, *a.shape[3:]), 2, 0)

    xs = (chunks(q), chunks(k), chunks(v), chunks(i_pre), chunks(jax.nn.log_sigmoid(f_pre)))
    tri = jnp.tril(jnp.ones((M_CHUNK, M_CHUNK), dtype=bool))

    def step(carry, inp):
        C, n, m = carry
        qc, kc, vc, ic, fc = inp
        b = jnp.cumsum(fc, axis=-1)
        log_d = jnp.where(tri, b[..., :, None] - b[..., None, :] + ic[..., None, :], NEG)
        m_inter = b + m[..., None]
        m_t = jnp.maximum(log_d.max(-1), m_inter)
        w_inter = jnp.exp(m_inter - m_t)
        s = jnp.einsum('bhtd,bhsd->bhts', qc, kc) * jnp.exp(log_d - m_t[..., None])
        num = jnp.einsum('bhts,bhsv->bhtv', s, vc) + w_inter[..., None] * jnp.einsum('bhtd,bhdv->bhtv', qc, C)
        den = s.sum(-1) + w_inter * jnp.einsum('bhtd,bhd->bht', qc, n)
        h = num / jnp.maximum(jnp.abs(den), jnp.exp(-m_t))[..., None]
        b_last = b[..., -1]
        log_w = b_last[..., None] - b + ic
        m_new = jnp.maximum(b_last + m, log_w.max(-1))
        w_state = jnp.exp(log_w - m_new[..., None])
        decay = jnp.exp(b_last + m - m_new)
        C = decay[..., None, None] * C + jnp.einsum('bhs,bhsd,bhsv->bhdv', w_state, kc, vc)
        n = decay[..., None] * n + jnp.einsum('bhs,bhsd->bhd', w_state, kc)
        return (C, n, m_new), h

    init = (jnp.zeros((B, H, dk, dv), jnp.float32), jnp.zeros((B, H, dk), jnp.float32),
            jnp.full((B, H), NEG, jnp.float32))
    _, h = lax.scan(step, init, xs)
    return jnp.moveaxis(h, 0, 2).reshape(B, H, S, dv)

def mlstm_branch(qk, v, o_pre, gate_pre, b_gates, conv_w, conv_b, gn_w):
    B, S, _ = v.shape
    f32 = jnp.float32
    qk = jax.nn.silu(centred_dwconv(qk, conv_w.astype(qk.dtype), conv_b.astype(qk.dtype)))

    def heads(a):
        return a.astype(f32).reshape(B, S, M_HEADS, M_HEAD_DIM).transpose(0, 2, 1, 3)

    q, k = jnp.split(qk, 2, axis=-1)
    q = heads(q) * M_HEAD_DIM ** -0.5
    k = heads(k)
    vh = heads(v)
    g = (gate_pre.astype(f32) + b_gates.astype(f32)).reshape(B, S, 4, M_HEADS).transpose(2, 0, 3, 1)
    i_f, f_f, i_b, f_b = g[0], g[1], g[2], g[3]
    flip = lambda a: jnp.flip(a, axis=2)
    h = mlstm_scan(q, k, vh, i_f, f_f) + flip(mlstm_scan(flip(q), flip(k), flip(vh), flip(i_b), flip(f_b)))
    mu = h.mean(-1, keepdims=True)
    var = jnp.square(h - mu).mean(-1, keepdims=True)
    hn = ((h - mu) * lax.rsqrt(var + LN_EPS)).transpose(0, 2, 1, 3).reshape(B, S, M_WIDTH)
    return (jax.nn.sigmoid(o_pre.astype(f32)) * hn * gn_w.astype(f32)).astype(v.dtype)

def banded_attention(q, k, v, slopes, dil, half):
    B, H, G, n, dh = q.shape
    nb = -(-n // half)
    n_pad = nb * half
    pad0 = ((0, 0),) * 3
    qb = jnp.pad(q, pad0 + ((0, n_pad - n), (0, 0))).reshape(B, H, G, nb, half, dh)

    def kblocks(a):
        ap = jnp.pad(a, pad0 + ((half, n_pad - n + half), (0, 0))).reshape(B, H, G, nb + 2, half, dh)
        return jnp.concatenate([ap[:, :, :, :-2], ap[:, :, :, 1:-1], ap[:, :, :, 2:]], axis=-2)

    kb, vb = kblocks(k), kblocks(v)
    qi = jnp.arange(n_pad).reshape(nb, half)
    kj = (jnp.arange(nb) * half - half)[:, None] + jnp.arange(3 * half)[None, :]
    dist = jnp.abs(qi[:, :, None] - kj[:, None, :])
    valid = (dist <= half) & (kj[:, None, :] >= 0) & (kj[:, None, :] < n)
    bias = -slopes[:, None, None, None] * (dil * dist).astype(jnp.float32)
    s = jnp.einsum('bhgnqd,bhgnkd->bhgnqk', qb, kb) * ATT_HEAD_DIM ** -0.5 + bias[None, :, None]
    s = jnp.where(valid, s, NEG)
    lse = jax.nn.logsumexp(s, axis=-1)
    o = jnp.einsum('bhgnqk,bhgnkd->bhgnqd', jnp.exp(s - lse[..., None]), vb)
    return o.reshape(B, H, G, n_pad, dh)[:, :, :, :n], lse.reshape(B, H, G, n_pad)[:, :, :, :n]

def dilated_attention(qkv, slopes):
    B, S, _ = qkv.shape
    qkv = qkv.astype(jnp.float32).reshape(B, S, 3, N_PATTERNS, ATT_SLOTS, ATT_HEAD_DIM)
    outs, lses = [], []
    for g, (win, dil) in enumerate(ATT_PATTERNS):
        n = S // dil

        def to_res(a):
            return a.reshape(B, n, dil, ATT_SLOTS, ATT_HEAD_DIM).transpose(0, 3, 2, 1, 4)

        o, lse = banded_attention(to_res(qkv[:, :, 0, g]), to_res(qkv[:, :, 1, g]),
                                  to_res(qkv[:, :, 2, g]), slopes[g], dil, win // (2 * dil))
        outs.append(o.transpose(0, 3, 2, 1, 4).reshape(B, S, ATT_SLOTS, ATT_HEAD_DIM))
        lses.append(lse.transpose(0, 3, 2, 1).reshape(B, S, ATT_SLOTS))
    w = jax.nn.softmax(jnp.stack(lses, axis=0), axis=0)
    o = (w[..., None] * jnp.stack(outs, axis=0)).sum(0)
    return o.reshape(B, S, ATT_OUT)

def mixer(u, w_in, b_gates, conv_w, conv_b, gn_w, w_a, w_b, w_out, slopes):
    z = u @ w_in
    idx = np.cumsum(IN_SECTIONS)[:-1].tolist()
    qk_m, v_m, o_m, gate_m, qkv_a, gates_br = jnp.split(z, idx, axis=-1)
    y_a = mlstm_branch(qk_m, v_m, o_m, gate_m, b_gates, conv_w, conv_b, gn_w) @ w_a
    y_b = dilated_attention(qkv_a, slopes).astype(u.dtype) @ w_b
    g_a, g_b = jnp.split(gates_br, 2, axis=-1)
    return (jax.nn.sigmoid(g_a) * y_a + jax.nn.sigmoid(g_b) * y_b) @ w_out

def swiglu(u, w1, w3, w2):
    return (jax.nn.silu(u @ w1) * (u @ w3)) @ w2

def first_inputs(seed: int = 0) -> dict:
    key = jax.random.key(seed)
    ks = jax.random.split(key, 24)

    def nrm(k, shape, scale):
        return jax.random.normal(k, shape, jnp.float32) * scale

    f_bias = jnp.linspace(3.0, 6.0, M_HEADS, dtype=jnp.float32)
    b_gates = jnp.concatenate([
        nrm(ks[3], (DEPTH, M_HEADS), 0.1),
        f_bias + nrm(ks[4], (DEPTH, M_HEADS), 0.1),
        nrm(ks[5], (DEPTH, M_HEADS), 0.1),
        f_bias + nrm(ks[6], (DEPTH, M_HEADS), 0.1)], axis=-1)
    return {
        "x": nrm(ks[0], (BATCH, SEQ, D_MODEL), 1.0),
        "c": nrm(ks[1], (BATCH, D_MODEL), 1.0),
        "w_in": nrm(ks[2], (DEPTH, D_MODEL, N_IN), D_MODEL ** -0.5),
        "b_gates": b_gates,
        "conv_w": nrm(ks[7], (DEPTH, CONV_WIDTH, 2 * M_WIDTH), CONV_WIDTH ** -0.5),
        "conv_b": nrm(ks[8], (DEPTH, 2 * M_WIDTH), 0.02),
        "gn_w": 1.0 + nrm(ks[9], (DEPTH, M_WIDTH), 0.02),
        "w_a": nrm(ks[10], (DEPTH, M_WIDTH, D_MODEL), M_WIDTH ** -0.5),
        "w_b": nrm(ks[11], (DEPTH, ATT_OUT, D_MODEL), ATT_OUT ** -0.5),
        "w_out": nrm(ks[12], (DEPTH, D_MODEL, D_MODEL), DN_BETA * D_MODEL ** -0.5),
        "w_ada": nrm(ks[13], (DEPTH, D_MODEL, 6 * D_MODEL), 0.5 * D_MODEL ** -0.5),
        "b_ada": nrm(ks[14], (DEPTH, 6 * D_MODEL), 0.02),
        "ln1_g": 1.0 + nrm(ks[15], (DEPTH, D_MODEL), 0.02),
        "ln1_b": nrm(ks[16], (DEPTH, D_MODEL), 0.02),
        "w1": nrm(ks[17], (DEPTH, D_MODEL, D_FF), D_MODEL ** -0.5),
        "w3": nrm(ks[18], (DEPTH, D_MODEL, D_FF), D_MODEL ** -0.5),
        "w2": nrm(ks[19], (DEPTH, D_FF, D_MODEL), DN_BETA * D_FF ** -0.5),
        "ln2_g": 1.0 + nrm(ks[20], (DEPTH, D_MODEL), 0.02),
        "ln2_b": nrm(ks[21], (DEPTH, D_MODEL), 0.02),
    }

def first_block(x, c, w_in, b_gates, conv_w, conv_b, gn_w, w_a, w_b, w_out, w_ada, b_ada,
              ln1_g, ln1_b, w1, w3, w2, ln2_g, ln2_b):
    slopes = alibi_slopes()
    c_act = jax.nn.silu(c)
    h = layer_norm(x)
    for l in range(DEPTH):
        ada = (c_act @ w_ada[l] + b_ada[l])[:, None, :]
        sh1, sc1, g1, sh2, sc2, g2 = jnp.split(ada, 6, axis=-1)
        u = h * (1.0 + sc1) + sh1
        y = mixer(u, w_in[l], b_gates[l], conv_w[l], conv_b[l], gn_w[l], w_a[l], w_b[l], w_out[l], slopes)
        h = layer_norm(DN_ALPHA * h + g1 * y, ln1_g[l], ln1_b[l])
        u = h * (1.0 + sc2) + sh2
        y = swiglu(u, w1[l], w3[l], w2[l])
        h = layer_norm(DN_ALPHA * h + g2 * y, ln2_g[l], ln2_b[l])
    return h


CTX_LEN = 256
GRID_W = 64
N_MIXERS = 4
MLP_HIDDEN = 4 * D_MODEL
N_MOD = 6
NORM_EPS = 1e-6
NEG_INF = -1e30

ATTN_HEADS = 16
ATTN_KV_HEADS = 4
ATTN_GROUP = ATTN_HEADS // ATTN_KV_HEADS
HEAD_DIM = D_MODEL // ATTN_HEADS
WINDOW = 128
ATTN_BLOCK = 128
ROPE_BASE = 10000.0
ROPE_AXIS_DIM = HEAD_DIM // 2
ROPE_FREQS = ROPE_AXIS_DIM // 2

GLA_HEADS = 4
GLA_KEY_DIM = D_MODEL // 2
GLA_VAL_DIM = D_MODEL
GLA_DK = GLA_KEY_DIM // GLA_HEADS
GLA_DV = GLA_VAL_DIM // GLA_HEADS
GLA_GATE_RANK = 16
GLA_TAU = 16.0
SCAN_CHUNK = 64

RWKV_HEAD_SIZE = 64
RWKV_HEADS = D_MODEL // RWKV_HEAD_SIZE
RWKV_DECAY_RANK = 64
RWKV_AAA_RANK = 64
RWKV_GATE_RANK = 128
RWKV_LN_EPS = 64e-5
L2_EPS = 1e-12

HGRN_EXPAND = 128
HGRN_HEADS = D_MODEL // HGRN_EXPAND
HGRN_FORGET_DIM = HGRN_HEADS * HGRN_EXPAND
HGRN_IN_DIM = D_MODEL // HGRN_HEADS

N_ATTN_LAYERS = (DEPTH + 3) // N_MIXERS
N_GLA_LAYERS = (DEPTH + 2) // N_MIXERS
N_RWKV_LAYERS = (DEPTH + 1) // N_MIXERS
N_HGRN_LAYERS = DEPTH // N_MIXERS


def rms_norm(x, gain):
    xf = x.astype(jnp.float32)
    y = xf * lax.rsqrt(jnp.mean(xf * xf, axis=-1, keepdims=True) + NORM_EPS)
    return (y * gain.astype(jnp.float32)).astype(x.dtype)

def modulate(x, gain, shift, scale):
    return rms_norm(x, gain) * (1 + scale) + shift

def channel_mlp(h, w_in, w_out):
    return jnp.square(jax.nn.relu(h @ w_in)) @ w_out

def axial_rope_tables(rows):
    inv_freq = ROPE_BASE ** (-jnp.arange(ROPE_FREQS, dtype=jnp.float32) * 2.0 / ROPE_AXIS_DIM)
    pos = jnp.arange(rows * GRID_W)
    row = (pos // GRID_W).astype(jnp.float32)
    col = (pos % GRID_W).astype(jnp.float32)
    ang = jnp.stack([row[:, None] * inv_freq, col[:, None] * inv_freq], axis=1)
    return jnp.cos(ang), jnp.sin(ang)

def apply_axial_rope(x, cos, sin):
    lead = x.shape[:-1]
    xr = x.reshape(lead + (2, 2, ROPE_FREQS))
    x1, x2 = xr[..., 0, :], xr[..., 1, :]
    bshape = (1, x.shape[1]) + (1,) * (x.ndim - 3) + cos.shape[1:]
    cb = cos.reshape(bshape).astype(x.dtype)
    sb = sin.reshape(bshape).astype(x.dtype)
    out = jnp.stack([x1 * cb - x2 * sb, x2 * cb + x1 * sb], axis=-2)
    return out.reshape(x.shape)

def softmax_with_sink(s, sink):
    sk = sink.astype(jnp.float32)[None, :, :, None, None]
    m = jnp.maximum(jnp.max(s, axis=-1, keepdims=True), sk)
    e = jnp.exp(s - m)
    return e / (jnp.sum(e, axis=-1, keepdims=True) + jnp.exp(sk - m))

def windowed_gqa_sink(h_lat, h_ctx, w_qkv, w_o, sink, cos, sin, need_ctx):
    B, L, _ = h_lat.shape
    nb = L // ATTN_BLOCK
    q_cols = ATTN_HEADS * HEAD_DIM
    kv_cols = ATTN_KV_HEADS * HEAD_DIM

    def project(h):
        T = h.shape[1]
        qkv = h @ w_qkv
        q = qkv[..., :q_cols].reshape(B, T, ATTN_KV_HEADS, ATTN_GROUP, HEAD_DIM) * (HEAD_DIM ** -0.5)
        k = qkv[..., q_cols:q_cols + kv_cols].reshape(B, T, ATTN_KV_HEADS, HEAD_DIM)
        v = qkv[..., q_cols + kv_cols:].reshape(B, T, ATTN_KV_HEADS, HEAD_DIM)
        return q, k, v

    q_lat, k_lat, v_lat = project(h_lat)
    q_ctx, k_ctx, v_ctx = project(h_ctx)
    q_lat = apply_axial_rope(q_lat, cos, sin)
    k_lat = apply_axial_rope(k_lat, cos, sin)
    sink_g = sink.reshape(ATTN_KV_HEADS, ATTN_GROUP)

    def band(t):
        tp = jnp.pad(t, ((0, 0), (ATTN_BLOCK, ATTN_BLOCK), (0, 0), (0, 0)))
        tp = tp.reshape(B, nb + 2, ATTN_BLOCK, ATTN_KV_HEADS, HEAD_DIM)
        return jnp.moveaxis(jnp.concatenate([tp[:, :-2], tp[:, 1:-1], tp[:, 2:]], axis=2), 1, 0)

    k_band, v_band = band(k_lat), band(v_lat)
    q_blocks = jnp.moveaxis(q_lat.reshape(B, nb, ATTN_BLOCK, ATTN_KV_HEADS, ATTN_GROUP, HEAD_DIM), 1, 0)
    n_loc = 3 * ATTN_BLOCK
    rel = jnp.arange(n_loc)[None, :] - ATTN_BLOCK - jnp.arange(ATTN_BLOCK)[:, None]
    in_window = jnp.abs(rel) <= WINDOW

    def attend_block(args):
        q, k, v, blk = args
        key_pos = blk * ATTN_BLOCK - ATTN_BLOCK + jnp.arange(n_loc)
        ok = in_window & ((key_pos >= 0) & (key_pos < L))[None, :]
        s_lat = jnp.einsum('bqhgd,bkhd->bhgqk', q, k).astype(jnp.float32)
        s_lat = jnp.where(ok, s_lat, NEG_INF)
        s_ctx = jnp.einsum('bqhgd,bkhd->bhgqk', q, k_ctx).astype(jnp.float32)
        p = softmax_with_sink(jnp.concatenate([s_lat, s_ctx], axis=-1), sink_g).astype(v.dtype)
        return (jnp.einsum('bhgqk,bkhd->bqhgd', p[..., :n_loc], v)
                + jnp.einsum('bhgqk,bkhd->bqhgd', p[..., n_loc:], v_ctx))

    o_lat = lax.map(attend_block, (q_blocks, k_band, v_band, jnp.arange(nb)))
    o_lat = jnp.moveaxis(o_lat, 0, 1).reshape(B, L, q_cols)
    y_lat = o_lat @ w_o
    if not need_ctx:
        return y_lat, None
    s_c = jnp.einsum('bqhgd,bkhd->bhgqk', q_ctx, k_ctx).astype(jnp.float32)
    p_c = softmax_with_sink(s_c, sink_g).astype(v_ctx.dtype)
    o_ctx = jnp.einsum('bhgqk,bkhd->bqhgd', p_c, v_ctx).reshape(B, h_ctx.shape[1], q_cols)
    return y_lat, o_ctx @ w_o

def reverse_segments(t, n_ctx):
    return jnp.concatenate([t[:, :n_ctx][:, ::-1], t[:, n_ctx:][:, ::-1]], axis=1)

def chunk_gated_scan(q, k, v, log_g):
    B, T, H, dk = q.shape
    dv = v.shape[-1]
    n = T // SCAN_CHUNK

    def chunks(t):
        return jnp.moveaxis(t.astype(jnp.float32).reshape(B, n, SCAN_CHUNK, H, t.shape[-1]), 1, 0)

    lower = jnp.tril(jnp.ones((SCAN_CHUNK, SCAN_CHUNK), dtype=bool))

    def step(S, xs):
        qc, kc, vc, gc = xs
        b = jnp.cumsum(gc, axis=1)
        q_dec = qc * jnp.exp(b)
        k_inv = kc * jnp.exp(-b)
        A = jnp.where(lower, jnp.einsum('bqhd,bkhd->bhqk', q_dec, k_inv), 0.0)
        o = jnp.einsum('bhqk,bkhv->bqhv', A, vc) + jnp.einsum('bqhd,bhdv->bqhv', q_dec, S)
        b_last = b[:, -1]
        k_end = kc * jnp.exp(b_last[:, None] - b)
        S = jnp.exp(b_last)[..., None] * S + jnp.einsum('bkhd,bkhv->bhdv', k_end, vc)
        return S, o

    S0 = jnp.zeros((B, H, dk, dv), jnp.float32)
    _, o = lax.scan(step, S0, (chunks(q), chunks(k), chunks(v), chunks(log_g)))
    return jnp.moveaxis(o, 0, 1).reshape(B, T, H, dv).astype(v.dtype)

def bidir_gated_scan(q, v, k_fwd, g_fwd, k_bwd, g_bwd, n_ctx):
    rev = lambda t: reverse_segments(t, n_ctx)
    o_f = chunk_gated_scan(q, k_fwd, v, g_fwd)
    o_b = chunk_gated_scan(rev(q), rev(k_bwd), rev(v), rev(g_bwd))
    return o_f + rev(o_b)

def gla_mixer(h_lat, h_ctx, w_in, w_gate_down, w_gate_up, gate_bias, g_norm, w_o, need_ctx):
    n_ctx = h_ctx.shape[1]
    h = jnp.concatenate([h_ctx, h_lat], axis=1)
    B, T, _ = h.shape
    z = h @ w_in
    q = z[..., :GLA_KEY_DIM].reshape(B, T, GLA_HEADS, GLA_DK) * (GLA_DK ** -0.5)
    k = z[..., GLA_KEY_DIM:2 * GLA_KEY_DIM].reshape(B, T, GLA_HEADS, GLA_DK)
    v = z[..., 2 * GLA_KEY_DIM:2 * GLA_KEY_DIM + GLA_VAL_DIM].reshape(B, T, GLA_HEADS, GLA_DV)
    out_gate = z[..., 2 * GLA_KEY_DIM + GLA_VAL_DIM:]

    def log_decay(d):
        zg = (h @ w_gate_down[d]) @ w_gate_up[d] + gate_bias[d]
        return (jax.nn.log_sigmoid(zg.astype(jnp.float32)) / GLA_TAU).reshape(B, T, GLA_HEADS, GLA_DK)

    o = bidir_gated_scan(q, v, k, log_decay(0), k, log_decay(1), n_ctx)
    o = rms_norm(o, g_norm).reshape(B, T, GLA_VAL_DIM) * jax.nn.silu(out_gate)
    y_lat = o[:, n_ctx:] @ w_o
    y_ctx = o[:, :n_ctx] @ w_o if need_ctx else None
    return y_lat, y_ctx

def centred_shift(h):
    hp = jnp.pad(h, ((0, 0), (1, 1), (0, 0)))
    return 0.5 * (hp[:, :-2] + hp[:, 2:]) - h

def rwkv7_scan(r, decay, kk, a, k, v):
    B, T, H, N = r.shape

    def step(S, xs):
        r_t, w_t, kk_t, a_t, k_t, v_t = xs
        sa = jnp.einsum('bhvk,bhk->bhv', S, -kk_t)
        S = (S * w_t[:, :, None, :] + sa[..., None] * (kk_t * a_t)[:, :, None, :]
             + v_t[..., None] * k_t[:, :, None, :])
        return S, jnp.einsum('bhvk,bhk->bhv', S, r_t)

    tm = lambda t: jnp.moveaxis(t.astype(jnp.float32), 1, 0)
    S0 = jnp.zeros((B, H, N, N), jnp.float32)
    _, y = lax.scan(step, S0, (tm(r), tm(decay), tm(kk), tm(a), tm(k), tm(v)))
    return jnp.moveaxis(y, 0, 1)

def rwkv7_mixer(h_lat, h_ctx, mix, w_rkv, w0, w_down, w_up, a0, a_down, a_up, g_down, g_up,
                k_k, k_a, r_k, ln_w, ln_b, w_o, need_ctx):
    n_ctx = h_ctx.shape[1]
    h = jnp.concatenate([h_ctx, h_lat], axis=1)
    dx = jnp.concatenate([centred_shift(h_ctx), centred_shift(h_lat)], axis=1)
    B, T, D = h.shape
    hm = h[None] + dx[None] * mix[:, None, None, :]
    r, k, v = jnp.einsum('nbtd,nde->nbte', hm[:3], w_rkv)
    hw, ha, hg = hm[3], hm[4], hm[5]
    heads = lambda t: t.reshape(B, T, RWKV_HEADS, RWKV_HEAD_SIZE)
    g = jax.nn.sigmoid(hg @ g_down) @ g_up
    kk = heads((k * k_k).astype(jnp.float32))
    kk = kk / jnp.maximum(jnp.sqrt(jnp.sum(kk * kk, axis=-1, keepdims=True)), L2_EPS)

    def direction(d):
        w_log = -jax.nn.softplus(-(w0[d] + jnp.tanh(hw @ w_down[d]) @ w_up[d]).astype(jnp.float32)) - 0.5
        a = jax.nn.sigmoid((a0[d] + (ha @ a_down[d]) @ a_up[d]).astype(jnp.float32))
        return heads(jnp.exp(-jnp.exp(w_log))), heads(a), heads(k * (1 + (a - 1) * k_a))

    dec_f, a_f, k_f = direction(0)
    dec_b, a_b, k_b = direction(1)
    r_h, v_h = heads(r), heads(v)
    rev = lambda t: reverse_segments(t, n_ctx)
    y = (rwkv7_scan(r_h, dec_f, kk, a_f, k_f, v_h)
         + rev(rwkv7_scan(rev(r_h), rev(dec_b), rev(kk), rev(a_b), rev(k_b), rev(v_h))))
    mu = jnp.mean(y, axis=-1, keepdims=True)
    var = jnp.mean(jnp.square(y - mu), axis=-1, keepdims=True)
    yn = ((y - mu) * lax.rsqrt(var + RWKV_LN_EPS) * ln_w.reshape(RWKV_HEADS, RWKV_HEAD_SIZE)
          + ln_b.reshape(RWKV_HEADS, RWKV_HEAD_SIZE))
    bonus = jnp.sum(r_h * (0.5 * (k_f + k_b)) * r_k, axis=-1, keepdims=True) * v_h
    out = (yn + bonus).reshape(B, T, D).astype(h.dtype) * g
    y_lat = out[:, n_ctx:] @ w_o
    y_ctx = out[:, :n_ctx] @ w_o if need_ctx else None
    return y_lat, y_ctx

def hgrn_lower_bound(lb_param, layer):
    p = jax.nn.softmax(lb_param.astype(jnp.float32), axis=0)
    return (jnp.cumsum(p, axis=0) - p[0])[layer]

def hgrn2_mixer(h_lat, h_ctx, w_in, w_f, lower_bound, g_norm, w_o, need_ctx):
    n_ctx = h_ctx.shape[1]
    h = jnp.concatenate([h_ctx, h_lat], axis=1)
    B, T, _ = h.shape
    z = h @ w_in
    q = jax.nn.silu(z[..., :HGRN_FORGET_DIM]).reshape(B, T, HGRN_HEADS, HGRN_EXPAND)
    i_in = z[..., HGRN_FORGET_DIM:HGRN_FORGET_DIM + D_MODEL].reshape(B, T, HGRN_HEADS, HGRN_IN_DIM)
    out_gate = z[..., HGRN_FORGET_DIM + D_MODEL:]

    def gates(d):
        f = lower_bound + (1 - lower_bound) * jax.nn.sigmoid((h @ w_f[d]).astype(jnp.float32))
        f = f.reshape(B, T, HGRN_HEADS, HGRN_EXPAND)
        return 1 - f, jnp.log(f)

    k_fwd, g_fwd = gates(0)
    k_bwd, g_bwd = gates(1)
    o = bidir_gated_scan(q, i_in, k_fwd, g_fwd, k_bwd, g_bwd, n_ctx)
    o = rms_norm(o, g_norm).reshape(B, T, D_MODEL) * jax.nn.silu(out_gate)
    y_lat = o[:, n_ctx:] @ w_o
    y_ctx = o[:, :n_ctx] @ w_o if need_ctx else None
    return y_lat, y_ctx

def second_inputs(seed: int = 0) -> dict:
    key = jax.random.key(seed)
    keys = iter(jax.random.split(key, 48))
    D = D_MODEL

    def normal(shape, scale):
        return jax.random.normal(next(keys), shape, jnp.float32) * scale

    def gain(shape):
        return 1.0 + normal(shape, 0.02)

    nA, nB, nC, nH = N_ATTN_LAYERS, N_GLA_LAYERS, N_RWKV_LAYERS, N_HGRN_LAYERS
    return {
        "x": normal((BATCH, SEQ, D), 1.0),
        "c": normal((BATCH, D), 1.0),
        "ctx": normal((BATCH, CTX_LEN, D), 1.0),
        "c_ctx": normal((D,), 1.0),
        "w_mod": normal((DEPTH, D, N_MOD * D), 0.5 * D ** -0.5),
        "b_mod": normal((DEPTH, N_MOD * D), 0.01),
        "g_pre_mix": gain((DEPTH, D)),
        "g_post_mix": gain((DEPTH, D)),
        "g_pre_mlp": gain((DEPTH, D)),
        "g_post_mlp": gain((DEPTH, D)),
        "w_mlp_in": normal((DEPTH, D, MLP_HIDDEN), D ** -0.5),
        "w_mlp_out": normal((DEPTH, MLP_HIDDEN, D), MLP_HIDDEN ** -0.5),
        "attn_w_qkv": normal((nA, D, (ATTN_HEADS + 2 * ATTN_KV_HEADS) * HEAD_DIM), D ** -0.5),
        "attn_w_o": normal((nA, ATTN_HEADS * HEAD_DIM, D), (ATTN_HEADS * HEAD_DIM) ** -0.5),
        "attn_sink": normal((nA, ATTN_HEADS), 0.5),
        "gla_w_in": normal((nB, D, 2 * GLA_KEY_DIM + 2 * GLA_VAL_DIM), D ** -0.5),
        "gla_w_gate_down": normal((nB, 2, D, GLA_GATE_RANK), D ** -0.5),
        "gla_w_gate_up": normal((nB, 2, GLA_GATE_RANK, GLA_KEY_DIM), GLA_GATE_RANK ** -0.5),
        "gla_gate_bias": normal((nB, 2, GLA_KEY_DIM), 0.1),
        "gla_g_norm": gain((nB, GLA_DV)),
        "gla_w_o": normal((nB, GLA_VAL_DIM, D), GLA_VAL_DIM ** -0.5),
        "rwkv_mix": jax.random.uniform(next(keys), (nC, 6, D), jnp.float32),
        "rwkv_w_rkv": normal((nC, 3, D, D), D ** -0.5),
        "rwkv_w0": -1.5 + normal((nC, 2, D), 0.5),
        "rwkv_w_down": normal((nC, 2, D, RWKV_DECAY_RANK), D ** -0.5),
        "rwkv_w_up": normal((nC, 2, RWKV_DECAY_RANK, D), 0.1 * RWKV_DECAY_RANK ** -0.5),
        "rwkv_a0": normal((nC, 2, D), 0.1),
        "rwkv_a_down": normal((nC, 2, D, RWKV_AAA_RANK), D ** -0.5),
        "rwkv_a_up": normal((nC, 2, RWKV_AAA_RANK, D), RWKV_AAA_RANK ** -0.5),
        "rwkv_g_down": normal((nC, D, RWKV_GATE_RANK), D ** -0.5),
        "rwkv_g_up": normal((nC, RWKV_GATE_RANK, D), RWKV_GATE_RANK ** -0.5),
        "rwkv_k_k": 0.85 + normal((nC, D), 0.02),
        "rwkv_k_a": gain((nC, D)),
        "rwkv_r_k": normal((nC, RWKV_HEADS, RWKV_HEAD_SIZE), 0.1),
        "rwkv_ln_w": gain((nC, D)),
        "rwkv_ln_b": normal((nC, D), 0.02),
        "rwkv_w_o": normal((nC, D, D), D ** -0.5),
        "hgrn_w_in": normal((nH, D, HGRN_FORGET_DIM + 2 * D), D ** -0.5),
        "hgrn_w_f": normal((nH, 2, D, HGRN_FORGET_DIM), D ** -0.5),
        "hgrn_lb": normal((DEPTH, HGRN_FORGET_DIM), 0.1),
        "hgrn_g_norm": gain((nH, HGRN_IN_DIM)),
        "hgrn_w_o": normal((nH, D, D), D ** -0.5),
    }

def second_block(x, c, ctx, c_ctx, w_mod, b_mod, g_pre_mix, g_post_mix, g_pre_mlp, g_post_mlp,
              w_mlp_in, w_mlp_out, attn_w_qkv, attn_w_o, attn_sink,
              gla_w_in, gla_w_gate_down, gla_w_gate_up, gla_gate_bias, gla_g_norm, gla_w_o,
              rwkv_mix, rwkv_w_rkv, rwkv_w0, rwkv_w_down, rwkv_w_up, rwkv_a0, rwkv_a_down,
              rwkv_a_up, rwkv_g_down, rwkv_g_up, rwkv_k_k, rwkv_k_a, rwkv_r_k, rwkv_ln_w,
              rwkv_ln_b, rwkv_w_o, hgrn_w_in, hgrn_w_f, hgrn_lb, hgrn_g_norm, hgrn_w_o):
    n_latent = x.shape[1]
    rows = n_latent // GRID_W
    cos, sin = axial_rope_tables(rows)
    c_lat = jax.nn.silu(c)
    c_con = jax.nn.silu(c_ctx)
    x_lat, x_ctx = x, ctx
    for i in range(DEPTH):
        kind, j = i % N_MIXERS, i // N_MIXERS
        need_ctx = i < DEPTH - 1
        m_lat = jnp.split((c_lat @ w_mod[i] + b_mod[i])[:, None, :], N_MOD, axis=-1)
        m_ctx = jnp.split(c_con @ w_mod[i] + b_mod[i], N_MOD, axis=-1)
        h_lat = modulate(x_lat, g_pre_mix[i], m_lat[0], m_lat[1])
        h_ctx = modulate(x_ctx, g_pre_mix[i], m_ctx[0], m_ctx[1])
        if kind == 0:
            y_lat, y_ctx = windowed_gqa_sink(h_lat, h_ctx, attn_w_qkv[j], attn_w_o[j], attn_sink[j],
                                             cos, sin, need_ctx)
        elif kind == 1:
            y_lat, y_ctx = gla_mixer(h_lat, h_ctx, gla_w_in[j], gla_w_gate_down[j], gla_w_gate_up[j],
                                     gla_gate_bias[j], gla_g_norm[j], gla_w_o[j], need_ctx)
        elif kind == 2:
            y_lat, y_ctx = rwkv7_mixer(h_lat, h_ctx, rwkv_mix[j], rwkv_w_rkv[j], rwkv_w0[j],
                                       rwkv_w_down[j], rwkv_w_up[j], rwkv_a0[j], rwkv_a_down[j],
                                       rwkv_a_up[j], rwkv_g_down[j], rwkv_g_up[j], rwkv_k_k[j],
                                       rwkv_k_a[j], rwkv_r_k[j], rwkv_ln_w[j], rwkv_ln_b[j],
                                       rwkv_w_o[j], need_ctx)
        else:
            y_lat, y_ctx = hgrn2_mixer(h_lat, h_ctx, hgrn_w_in[j], hgrn_w_f[j],
                                       hgrn_lower_bound(hgrn_lb, i), hgrn_g_norm[j], hgrn_w_o[j],
                                       need_ctx)
        x_lat = x_lat + m_lat[2] * rms_norm(y_lat, g_post_mix[i])
        f_lat = channel_mlp(modulate(x_lat, g_pre_mlp[i], m_lat[3], m_lat[4]), w_mlp_in[i], w_mlp_out[i])
        x_lat = x_lat + m_lat[5] * rms_norm(f_lat, g_post_mlp[i])
        if need_ctx:
            x_ctx = x_ctx + m_ctx[2] * rms_norm(y_ctx, g_post_mix[i])
            f_ctx = channel_mlp(modulate(x_ctx, g_pre_mlp[i], m_ctx[3], m_ctx[4]), w_mlp_in[i], w_mlp_out[i])
            x_ctx = x_ctx + m_ctx[5] * rms_norm(f_ctx, g_post_mlp[i])
    return x_lat


def setup_inputs(seed=0):
    out = dict(first_inputs(seed))
    for name, value in second_inputs(seed + 1).items():
        if name != "x":
            out[name + "_2"] = value
    return out


def reference(
    x, c, w_in, b_gates, conv_w, conv_b, gn_w, w_a, w_b, w_out, w_ada, b_ada, ln1_g, ln1_b, w1,
    w3, w2, ln2_g, ln2_b, c_2, ctx_2, c_ctx_2, w_mod_2, b_mod_2, g_pre_mix_2, g_post_mix_2,
    g_pre_mlp_2, g_post_mlp_2, w_mlp_in_2, w_mlp_out_2, attn_w_qkv_2, attn_w_o_2, attn_sink_2,
    gla_w_in_2, gla_w_gate_down_2, gla_w_gate_up_2, gla_gate_bias_2, gla_g_norm_2, gla_w_o_2,
    rwkv_mix_2, rwkv_w_rkv_2, rwkv_w0_2, rwkv_w_down_2, rwkv_w_up_2, rwkv_a0_2, rwkv_a_down_2,
    rwkv_a_up_2, rwkv_g_down_2, rwkv_g_up_2, rwkv_k_k_2, rwkv_k_a_2, rwkv_r_k_2, rwkv_ln_w_2,
    rwkv_ln_b_2, rwkv_w_o_2, hgrn_w_in_2, hgrn_w_f_2, hgrn_lb_2, hgrn_g_norm_2, hgrn_w_o_2,
):
    x = first_block(
        x, c, w_in, b_gates, conv_w, conv_b, gn_w, w_a, w_b, w_out, w_ada, b_ada, ln1_g, ln1_b,
        w1, w3, w2, ln2_g, ln2_b,
    )
    return second_block(
        x, c_2, ctx_2, c_ctx_2, w_mod_2, b_mod_2, g_pre_mix_2, g_post_mix_2, g_pre_mlp_2,
        g_post_mlp_2, w_mlp_in_2, w_mlp_out_2, attn_w_qkv_2, attn_w_o_2, attn_sink_2,
        gla_w_in_2, gla_w_gate_down_2, gla_w_gate_up_2, gla_gate_bias_2, gla_g_norm_2,
        gla_w_o_2, rwkv_mix_2, rwkv_w_rkv_2, rwkv_w0_2, rwkv_w_down_2, rwkv_w_up_2, rwkv_a0_2,
        rwkv_a_down_2, rwkv_a_up_2, rwkv_g_down_2, rwkv_g_up_2, rwkv_k_k_2, rwkv_k_a_2,
        rwkv_r_k_2, rwkv_ln_w_2, rwkv_ln_b_2, rwkv_w_o_2, hgrn_w_in_2, hgrn_w_f_2, hgrn_lb_2,
        hgrn_g_norm_2, hgrn_w_o_2,
    )


_drawn_inputs = setup_inputs


def setup_inputs(seed=0):
    import zlib

    import numpy as np

    out = dict(_drawn_inputs(seed))
    spreads = {}
    factors = {'conv_w': 5.326,
     'conv_b': 58.199,
     'gn_w': 8.0,
     'b_ada': 5.21,
     'g_pre_mix_2': 4.575,
     'g_post_mix_2': 6.206,
     'g_pre_mlp_2': 6.005,
     'g_post_mlp_2': 6.824,
     'attn_sink_2': 8.0,
     'gla_gate_bias_2': 3.632,
     'gla_g_norm_2': 40.021}
    for name, (base, spread) in spreads.items():
        noise = np.random.default_rng([zlib.crc32(name.encode()), seed]).standard_normal(out[name].shape)
        drawn = base * np.exp(spread * noise) if base else spread * noise
        out[name] = jnp.asarray(drawn.astype(out[name].dtype))
    for name, factor in factors.items():
        out[name] = (out[name] * factor).astype(out[name].dtype)
    return out
```

```python
import concourse.bass as bass
import concourse.mybir as mybir
import numpy as np
from contextlib import ExitStack

F32 = mybir.dt.float32
ALU = mybir.AluOpType
ACT = mybir.ActivationFunctionType
AX = mybir.AxisListType

P = 128
D = 1024
KD = D // P
T = 256
NT = T // P
DEPTH = 2
PW = 512
LN_EPS = 1e-5
RMS_EPS = 1e-6
ALPHA = float((2 * DEPTH) ** 0.25)
NEG = -1e30

M_HEADS, M_DIM = 4, 256
M_WIDTH = M_HEADS * M_DIM
TAPS = 5
SLOTS, A_DIM, PATTERNS = 8, 64, ((128, 1), (512, 4), (2048, 16))
NPAT = len(PATTERNS)
A_WIDTH = NPAT * SLOTS * A_DIM
A_OUT = SLOTS * A_DIM
D_FF = 2816
FFT = D_FF // P
COL_V = 2 * M_WIDTH
COL_O = COL_V + M_WIDTH
COL_GATE = COL_O + M_WIDTH
COL_A = COL_GATE + 4 * M_HEADS
COL_GB = COL_A + 3 * A_WIDTH
SLOPES = np.exp2(-8.0 * np.arange(1, NPAT * SLOTS + 1, dtype=np.float32) / (NPAT * SLOTS)).astype(np.float32).reshape(NPAT, SLOTS)

RING = 4
HP = 256
ADA_SLOTS, ACC_SLOTS = 2, 4
ADA_LATER = [8 + i for i in range(16)]
ADA_HEADS = [1, 5, 9, 13]
ADA_TAIL = list(range(20, 24))
ADA_NEXT = list(range(8))


def layer_panels():
    out = [("w_in", 0, KD, PW * i, PW) for i in range(4)]
    out += [("w_in", 0, KD, COL_O + PW * i, PW) for i in range(2)]
    out += [("w_in", 0, KD, COL_V + PW * i, PW) for i in range(2)]
    out += [("w_in", 0, KD, COL_A + PW * i, PW) for i in range(6)]
    out += [("w_in", 0, KD, COL_A + 2 * A_WIDTH + PW * i, PW) for i in range(3)]
    for i in range(2):
        out += [("w_in", 0, KD, COL_GB + PW * i, PW), ("w_in", 0, KD, COL_GB + D + PW * i, PW),
                ("w_a", 0, KD, PW * i, PW), ("w_b", 0, A_OUT // P, PW * i, PW)]
    out += [("w_out", 0, KD, PW * i, PW) for i in range(2)]
    for i in range(-(-D_FF // PW)):
        w = min(PW, D_FF - PW * i)
        out += [("w1", 0, KD, PW * i, w), ("w3", 0, KD, PW * i, w)]
    for half in range(2):
        out += [("w2", k, min(KD, FFT - k), PW * half, PW) for k in range(0, FFT, KD)]
    return out


LAYER_PANELS = layer_panels()
LAYER_SLOTS = -(-len(LAYER_PANELS) // RING) * RING


HEADS, KV, HD = 16, 4, 64
WINDOW, GRID_W, ROPE_BASE = 128, 64, 10000.0
G_HEADS, G_DK, G_DV, G_CHUNK, G_TAU = 4, 128, 256, 64, 16.0
MLP = 4 * D
MT = MLP // P
MLP_PANELS = [("w_mlp_in", 0, KD, PW * i, PW) for i in range(MLP // PW)] + \
             [("w_mlp_out", KD * k, KD, PW * half, PW) for half in range(2) for k in range(MT // KD)]
ATTN_PANELS = [("w_qkv", 0, KD, PW * i, PW) for i in range(3)] + [("w_o", 0, KD, PW * i, PW) for i in range(2)] + MLP_PANELS
GLA_PANELS = [("w_gla", 0, KD, PW * i, PW) for i in (4, 5, 2, 3, 1, 0)] + [("w_gla_o", 0, KD, PW * i, PW) for i in range(2)] + MLP_PANELS
TAIL_PANELS = [(0, *p) for p in ATTN_PANELS] + [(1 if p[0].startswith("w_mlp") else 0, *p) for p in GLA_PANELS]


def second_constants():
    f = np.float32
    i = np.arange(P)
    rot = np.zeros((P, P))
    first = (i % 32) < 16
    rot[i[first] + 16, i[first]] = -1.0
    rot[i[~first] - 16, i[~first]] = 1.0
    inv = (f(ROPE_BASE) ** (-np.arange(16, dtype=f) * f(2.0) / f(32))).astype(f)
    pos = np.arange(T)
    axis = np.stack([pos // GRID_W, pos % GRID_W]).astype(f)
    ang = axis[(i % 64) // 32] * inv[i % 16][:, None]
    t = i[:, None, None] + P * np.arange(NT)[None, :, None]
    s = np.arange(2 * T)[None, None, :]
    band = np.where((s >= T) | (np.abs(t - s) <= WINDOW), 0.0, NEG)
    attn = [rot, np.cos(ang), np.sin(ang), band]
    k, q = i[:, None], i[None, :]
    same = (k // G_CHUNK) == (q // G_CHUNK)
    gla = [same & (k <= q), (k // G_CHUNK) < (q // G_CHUNK), same & (k >= q), (k // G_CHUNK) > (q // G_CHUNK)]
    keep = np.ones((P, 2 * T))
    keep[:, 0:T:G_CHUNK] = 0.0
    keep[:, T] = 0.0
    flat = lambda parts: np.concatenate([np.asarray(a, f).reshape(P, -1) for a in parts], axis=1)
    return flat(attn), flat([*gla, keep])


NP2 = 4 * KD + HEADS + 2 + 8 + KD * 64 + 512
NC2 = P + 2 * T + NT * 2 * T


def first_constants():
    i = np.arange(P)
    ident = np.eye(P)
    ones = np.ones((P, P))
    upper = (i[:, None] <= i[None, :])
    lower = (i[:, None] >= i[None, :])
    t = i[:, None, None] + P * np.arange(NT)[None, :, None]
    s = np.arange(T)[None, None, :]
    past = np.where(s <= t, 0.0, NEG)
    future = np.where(s >= t, 0.0, NEG)
    dist = []
    for win, dil in PATTERNS:
        seen = (np.abs(t - s) <= dil * (win // (2 * dil))) & ((t - s) % dil == 0)
        dist.append(np.where(seen, -np.abs(t - s), NEG))
    parts = [ident, ones, upper, lower, past, future, *dist]
    return np.concatenate([a.reshape(P, -1) for a in parts], axis=1).astype(np.float32)


def memory(sizes):
    at, out = 0, {}
    for name, n in sizes:
        out[name] = at
        at += n
    return out, at


NCST = 4 * P + 2 * NT * T + NPAT * NT * T
NPAR = 16 * TAPS + 16 + KD + 16 + KD * 16 + 4 * KD


M, ARENA = memory([("RING", RING * KD * PW), ("ADAW", ADA_SLOTS * (KD + 1) * HP), ("ACC", ACC_SLOTS * HP), ("CST", NCST),
                   ("CSIL", 5 * KD), ("ADAC", 6 * KD), ("ADACX", 6 * KD), ("COLS", 3 * KD), ("GROW", 2 * D), ("H", NT * D), ("PAR", NPAR),
                   ("STAT", 32), ("GATE", 288), ("UT", KD * T), ("QK", 16 * T), ("SIG", KD * T), ("AQ", 12 * T),
                   ("AK", 12 * T), ("VM", NT * M_WIDTH), ("VA", NT * A_WIDTH), ("WORK", 12 * T)])


M2, ARENA2 = memory([("X", 4 * D), ("SM2", 384), ("UT2", KD * 2 * T), ("GT2", 32 * 2 * T + 320)])
M2 = {k: v + M["H"] for k, v in M2.items()}
ARENA = max(ARENA, ARENA2 + M["H"])


def minis(n):
    return [(h, s) for h in range(M_HEADS) for s, lag in ((3, 5), (2, 4), (1, 3), (0, 1)) if n == 2 * h + lag]


class Progress:

    phase = ""

    def __init__(self, engine, marks):
        self.engine, self.marks, self.count = engine, marks, 0

    def step(self, name=None):
        self.count += 1
        if name is not None:
            self.marks[Progress.phase, self.engine, name] = self.count
        return 1

    def drained(self, key):
        if key is None:
            return self.step()
        self.marks[Progress.phase, "drainer", key] = self.engine
        return self.step(key + " drained")

    def at(self, name):
        return self.marks.get((Progress.phase, self.engine, name), 1)

    def start(self, phase):
        Progress.phase, self.count = phase, 0


def program(nc, a, out, marks):
    with ExitStack() as ctx:
        def sem(name):
            return ctx.enter_context(nc.semaphore(name))

        arena = ctx.enter_context(nc.sbuf_tensor("arena", [P, ARENA], F32))
        banks = [ctx.enter_context(nc.psum_tensor(f"bank{i}", [P, 512], F32)) for i in range(8)]

        pe_done, act_done, dve_done = sem("pe_done"), sem("act_done"), sem("dve_done")
        params_in, rows1_in, rows2_in = sem("params_in"), sem("rows1_in"), sem("rows2_in")
        panel_in = [sem(f"panel{i}_in") for i in range(RING)]
        panels_free = sem("panels_free")
        ada_in = [sem(f"ada{i}_in") for i in range(ADA_SLOTS)]
        ada_free = sem("ada_free")
        phase_end, phase_go, phase_seen = sem("phase_end"), sem("phase_go"), sem("phase_seen")
        x_in, cst_in, out_done = sem("x_in"), sem("cst_in"), sem("out_done")
        ctx_in, par2_in = sem("ctx_in"), sem("par2_in")

        PE, AC, DV = (Progress(n, marks) for n in ("pe", "act", "dve"))

        def area(start, *shape):
            n = int(np.prod(shape))
            v = arena[:, start:start + n]
            if len(shape) == 1:
                return v
            names = "abcd"[:len(shape)]
            return v.rearrange(f"p ({' '.join(names)}) -> p {' '.join(names)}", **dict(zip(names, shape)))

        ring = area(M["RING"], RING, KD, PW)
        adaw = area(M["ADAW"], ADA_SLOTS, KD + 1, HP)
        acc = area(M["ACC"], ACC_SLOTS, HP)
        cst = area(M["CST"], NCST)
        ident, ones, upper, lower = (cst[:, P * i:P * i + P] for i in range(4))
        o = 4 * P
        past = area(M["CST"] + o, NT, T)
        masks = area(M["CST"] + o, 2, NT, T)
        dist = area(M["CST"] + o + 2 * NT * T, NPAT, NT * T)
        csil = area(M["CSIL"], 5, KD)
        adac = area(M["ADAC"], 6, KD)
        adacx = area(M["ADACX"], 6, KD)
        colA, colB, colT = (area(M["COLS"] + KD * i, KD) for i in range(3))
        grow = area(M["GROW"], 2, D)
        H = area(M["H"], NT, D)
        par = M["PAR"]
        conv_w = area(par, 16, TAPS)
        conv_b = area(par + 80, 16)
        gn_w = area(par + 96, KD)
        bg_row = area(par + 104, 16)
        w_gate = area(par + 120, KD, 16)
        ln_cols = area(par + 248, 4, KD)
        stats = area(M["STAT"], 24)
        mv = area(M["STAT"] + 24, NT, 2)
        rstd = area(M["STAT"] + 28, NT)
        UT = area(M["UT"], KD, T)
        QK = area(M["QK"], 16, T)
        SIG = area(M["SIG"], KD, T)
        AQ = area(M["AQ"], 12, T)
        AK = area(M["AK"], 12, T)
        GT = area(M["AQ"], FFT, T)
        VM = area(M["VM"], NT, M_WIDTH)
        rows = area(M["VM"], 2, D)
        VA = area(M["VA"], NT, A_WIDTH)
        MIX = area(M["VA"], KD, T)
        OAT = area(M["QK"] + 3072, A_OUT // P, T)
        SC = [area(M["QK"] + NT * NPAT * T * i, NT, NPAT * T) for i in range(2)]
        PT = area(M["WORK"], 2, 2 * NPAT, T)
        gz = area(M["GATE"], NT, 16)
        gw = area(M["GATE"] + 32, 4, 32)
        aB = area(M["GATE"] + 160, 2, 2, NT, 4)
        small = area(M["GATE"] + 192, 16, 4)
        W = M["WORK"]
        Am = area(W, 2, NT, T)
        Pm = area(W + 1024, NT, T)
        PTm = area(W + 1536, NT, T)
        hn = area(W + 2048, NT, T)
        diag = area(W + 2560, 4, P)
        cbuf = area(W, 4, T)
        sg = area(W, 4, 2 * T)
        lnt = area(W + 4 * PW, 2, PW)
        att = area(M["GATE"] + 256, 2, 4, NT)

        par2 = M["CST"] + 2 * P + NC2
        rot = area(M["CST"] + 2 * P, P)
        cosT, sinT = area(M["CST"] + 3 * P, T), area(M["CST"] + 3 * P + T, T)
        band = area(M["CST"] + 3 * P + 2 * T, NT, 2 * T)
        gmask = area(M["CST"] + 2 * P, 4 * P)
        keep = area(M["CST"] + 6 * P, 2 * T)
        gains = area(par2, 4, KD)
        sinks = area(par2 + 32, HEADS)
        g_norm = area(par2 + 48, 2)
        g_bias = area(par2 + 50, 2, G_HEADS)
        w_down = area(par2 + 58, KD, 64)
        w_up = area(par2 + 58 + KD * 64, 512)
        X = area(M2["X"], 4, D)
        sm = M2["SM2"]
        sink8 = area(sm, HEADS)
        ssq = area(sm + 16, 2, 4)
        rst = area(sm + 24, 4)
        aux1 = area(sm + 28, 4)
        colX = area(sm + 32, 2, KD)
        hst = area(sm + 48, 2, 6, 4)
        gst = area(sm + 96, 64)
        UT2 = area(M2["UT2"], KD, 2 * T)
        G0 = M2["GT2"]
        GT2 = area(G0, MT, 2 * T)
        GT2n = area(G0, MT, T)
        QT = area(G0, 8, 2 * T)
        KT = area(G0 + 4096, 2, 2 * T)
        VT = area(G0 + 5120, 4, T)
        SCA = [area(G0 + 6144 + 1536 * i, 1536) for i in range(2)]
        PTA = area(G0 + 9216, 2, 6, T)
        gKT = area(G0, G_HEADS, 2 * T)
        gQT = area(G0 + 2048, G_HEADS, T)
        gV = area(G0 + 3072, 4, D)
        gOT = area(G0 + 7168, KD, T)
        gDT = area(G0 + 9216, 2 * T)
        gZ, gL, gC = (area(G0 + 9728 + 512 * i, 2 * T) for i in range(3))
        g1 = G0 + 11264
        gQD, gKI, gQL = (area(g1 + 512 * i, 2, T) for i in range(3))
        gKE = area(g1 + 1536, 2, 2 * T)
        gKL = area(g1 + 2560, 2, P)
        gKK = area(g1 + 2816, 6, P)
        gAT = area(g1 + 3584, NT, P)
        gS = area(g1 + 3840, 2, 2, G_DV)
        gHN = area(g1 + 4864, NT, G_DV)
        gdec = area(sm + 160, 2, 8)

        def aux(at):
            return area(at, D), area(at + D, 4, P), area(at + D + 4 * P, 2, PW), area(at + 2 * D + 4 * P, D)

        
        def norm_places(tag):
            return aux({"attn": G0 + 12288, "gla": G0, "attn mlp": M2["UT2"], "gla mlp": M2["UT2"]}[tag])

        def tile(key):
            return banks[marks.get((Progress.phase, "bank", key), 0)]

        block = ctx.enter_context(nc.Block())

        @block.tensor
        def _(pe):
            st = {"n": 0, "panel": 0, "free": 0, "acc": 0}

            def open_tile(key):
                n = st["n"]
                st["n"] += 1
                marks[Progress.phase, "tenant", n] = key
                marks[Progress.phase, "bank", key] = n % 8
                if n >= 8:
                    old = marks[Progress.phase, "tenant", n - 8]
                    drained(old)
                return banks[n % 8]

            def mm(out, lhsT, rhs, start=True, stop=True, done=None, t=False):
                if t:
                    ins = nc.tensor.transpose(out, lhsT, rhs)
                else:
                    ins = nc.tensor.matmul(out, lhsT, rhs, start=start, stop=stop)
                if done:
                    ins.then_inc(pe_done, PE.step(done + " full"))
                elif st["free"]:
                    ins.then_inc(panels_free, st["free"])
                    st["free"] = 0

            def panel(l):
                n = st["panel"]
                st["panel"] += 1
                uses = [len([i for i in range(len(LAYER_PANELS)) if i % RING == s]) for s in range(RING)]
                s = n % RING
                pe.wait_ge(panel_in[s], l * (16 * uses[s]) + 16 * (n // RING + 1))
                return ring[:, s]

            def release(n=1):
                st["free"] += n

            def drained(key):
                who = marks.get((Progress.phase, "drainer", key))
                if who == "act":
                    pe.wait_ge(act_done, AC.at(key + " drained"))
                if who == "dve":
                    pe.wait_ge(dve_done, DV.at(key + " drained"))

            def feature_tiles(key, w, n, x, k=KD, cols=0):
                ps = open_tile(key)
                for j in range(2):
                    for i in range(k):
                        mm(ps[:, j * T:j * T + T], w[:, i, cols + (2 * n + j) * P:cols + (2 * n + j + 1) * P], x[:, i, :],
                           start=(i == 0), stop=(i == k - 1), done=key if j == 1 and i == k - 1 else None)

            def token_tile(key, w, tt, x, k=KD):
                ps = open_tile(key)
                for i in range(k):
                    mm(ps[:, :PW], x[:, i, tt * P:tt * P + P], w[:, i, :PW], start=(i == 0), stop=(i == k - 1),
                       done=key if i == k - 1 else None)

            def transposes(tag):
                for i in range(4):
                    key = f"{tag} {i}"
                    ps = open_tile(key)
                    for j in range(4):
                        ft, tt = 2 * i + j // 2, j % 2
                        mm(ps[:, j * P:j * P + P], H[:, tt, ft * P:ft * P + P], ident, t=True, done=key if j == 3 else None)

            def ada(tag, q):
                n = st["acc"]
                st["acc"] += 1
                key = f"{tag} {q}"
                ps = open_tile(key)
                pe.wait_ge(dve_done, DV.at(key + " acc"))
                x = acc[:, n % ACC_SLOTS, :]
                if q // 4 in (2, 5):
                    mm(ps[:, :HP], ones, x, done=key)
                else:
                    for c in range(2):
                        mm(ps[:, c * P:c * P + P], x[:, c * P:c * P + P], ones, done=key if c else None)

            def pe_mini(h, s):
                if s == 0:
                    pe.wait_ge(dve_done, DV.at(f"diag {h}"))
                    ps = open_tile(f"A {h}")
                    mm(ps[:, :], ones, diag[:, :, :].rearrange("p a b -> p (a b)"), done=f"A {h}")
                    pe.wait_ge(act_done, AC.at("silu 7"))
                    ps = open_tile(f"S {h}")
                    for tt in range(NT):
                        for i in range(2):
                            mm(ps[:, tt * T:tt * T + T], QK[:, 2 * h + i, tt * P:tt * P + P], QK[:, 8 + 2 * h + i, :],
                               start=(i == 0), stop=(i == 1), done=f"S {h}" if tt and i else None)
                elif s == 1:
                    pe.wait_ge(dve_done, DV.at(f"P {h}"))
                    ps = open_tile(f"PTT {h}")
                    for j in range(4):
                        mm(ps[:, j * P:j * P + P], Pm[:, j % 2, (j // 2) * P:(j // 2) * P + P], ident, t=True,
                           done=f"PTT {h}" if j == 3 else None)
                elif s == 2:
                    pe.wait_ge(act_done, AC.at(f"PTT {h} drained"))
                    if h == 0:
                        for n in range(4):
                            pe.wait_ge(act_done, AC.at(f"VM {n} drained"))
                    ps = open_tile(f"HV {h}")
                    for tt in range(NT):
                        for i in range(NT):
                            mm(ps[:, tt * T:tt * T + T], PTm[:, i, tt * P:tt * P + P], VM[:, i, h * M_DIM:(h + 1) * M_DIM],
                               start=(i == 0), stop=(i == 1), done=f"HV {h}" if tt and i else None)
                else:
                    pe.wait_ge(dve_done, DV.at(f"hn {h}"))
                    ps = open_tile(f"HT {h}")
                    for j in range(4):
                        mm(ps[:, j * P:j * P + P], hn[:, j % 2, (j // 2) * P:(j // 2) * P + P], ident, t=True,
                           done=f"HT {h}" if j == 3 else None)

            def phase_over():
                pe.wait_ge(pe_done, PE.count)
                pe.sem_inc(phase_end, 1)

            pe.sem_inc(panels_free, RING)
            PE.start("start")
            pe.wait_ge(cst_in, 16)
            for q in ADA_NEXT:
                ada("ada", q)
            phase_over()

            with pe.Fori(0, DEPTH) as l:
                pe.wait_ge(phase_go, l + 1)
                pe.sem_inc(phase_seen, 1)
                PE.start("layer")
                st.update(n=0, panel=0, acc=0)
                transposes("T")
                for i in range(4):
                    drained(f"T {i}")
                ps = open_tile("G")
                pe.wait_ge(params_in, 16)
                for tt in range(NT):
                    for i in range(KD):
                        mm(ps[:, tt * 16:tt * 16 + 16], UT[:, i, tt * P:tt * P + P], w_gate[:, i, :],
                           start=(i == 0), stop=(i == KD - 1), done="G" if tt == 1 and i == KD - 1 else None)
                for p in range(4):
                    w = panel(l)
                    for n in range(2):
                        feature_tiles(f"QK {2 * p + n}", w, n, UT)
                        if p == 0 and n == 1:
                            pe.wait_ge(dve_done, DV.at("lf"))
                            ps = open_tile("CS")
                            lf = gw[:, 3, :].rearrange("p (t g) -> p t g", t=NT)
                            jobs = [[(upper, 0)], [(ones, 0), (upper, 1)], [(lower, 0), (ones, 1)], [(lower, 1)]]
                            for j, terms in enumerate(jobs):
                                for i, (m, tt) in enumerate(terms):
                                    lastt = i == len(terms) - 1
                                    mm(ps[:, j * 16:j * 16 + 16], m, lf[:, tt, :], start=(i == 0), stop=lastt,
                                       done="CS" if j == 3 and lastt else None)
                    release()
                nj = 0
                for p in range(4):
                    w = panel(l)
                    for n in range(2):
                        if p < 2:
                            feature_tiles(f"O {2 * p + n}", w, n, UT)
                        else:
                            token_tile(f"VM {2 * (p - 2) + n}", w, n, UT)
                        if nj:
                            for q in ADA_LATER[2 * nj - 2:2 * nj]:
                                ada("ada", q)
                        nj += 1
                    release()
                for q in ADA_LATER[14:]:
                    ada("ada", q)
                for p in range(6):
                    w = panel(l)
                    for n in range(2):
                        feature_tiles(f"AQK {2 * p + n}", w, n, UT)
                        for h, s in minis(2 * p + n):
                            pe_mini(h, s)
                    release()
                for p in range(3):
                    w = panel(l)
                    for n in range(2):
                        token_tile(f"VA {2 * p + n}", w, n, UT)
                    release()
                for i in range(SLOTS + 1):
                    if i < SLOTS:
                        if i == 0:
                            for n in range(6, 12):
                                pe.wait_ge(act_done, AC.at(f"AQK {n} drained"))
                        p0 = A_DIM * (i % 2)
                        for g in range(NPAT):
                            key = f"SC {i} {g}"
                            ps = open_tile(key)
                            x = g * 4 + i // 2
                            for tt in range(NT):
                                mm(ps[:, tt * T:tt * T + T], AQ[p0:p0 + A_DIM, x, tt * P:tt * P + P],
                                   AK[p0:p0 + A_DIM, x, :], done=key if tt else None)
                    if i:
                        n = i - 1
                        pe.wait_ge(dve_done, DV.at(f"probs {n}"))
                        for g in range(NPAT):
                            key = f"PT {n} {g}"
                            ps = open_tile(key)
                            for j in range(4):
                                stt, tt = j // 2, j % 2
                                mm(ps[:, j * P:j * P + P], SC[n % 2][:, tt, g * T + stt * P:g * T + stt * P + P], ident,
                                   t=True, done=key if j == 3 else None)
                        if n == 0:
                            for j in range(6):
                                pe.wait_ge(act_done, AC.at(f"VA {j} drained"))
                        key = f"AV {n}"
                        ps = open_tile(key)
                        p0 = A_DIM * (n % 2)
                        for g in range(NPAT):
                            pe.wait_ge(act_done, AC.at(f"PT {n} {g} drained"))
                            for stt in range(2):
                                j = 2 * g + stt
                                mm(ps[p0:p0 + A_DIM, :T], VA[:, stt, g * A_OUT + n * A_DIM:g * A_OUT + (n + 1) * A_DIM],
                                   PT[:, n % 2, j, :], start=(j == 0), stop=(j == 5), done=key if j == 5 else None)
                for p in range(2):
                    for name in ("GA", "GB", "WA", "WB"):
                        w = panel(l)
                        if name == "WA":
                            pe.wait_ge(dve_done, DV.at("y_m"))
                        if name == "WB":
                            for n in range(SLOTS):
                                pe.wait_ge(act_done, AC.at(f"AV {n} drained"))
                        for n in range(2):
                            x, k = {"WA": (SIG, KD), "WB": (OAT, A_OUT // P)}.get(name, (UT, KD))
                            feature_tiles(f"{name} {2 * p + n}", w, n, x, k)
                        release()
                pe.wait_ge(dve_done, DV.at("mix 3"))
                for p in range(2):
                    w = panel(l)
                    for tt in range(NT):
                        token_tile(f"WO {p} {tt}", w, tt, MIX)
                    release()
                pe.wait_ge(dve_done, DV.at("ln1"))
                transposes("U")
                for i in range(4):
                    drained(f"U {i}")
                j = 0
                for p in range(6):
                    w1, w3 = panel(l), panel(l)
                    for n in range(2 if p < 5 else 1):
                        feature_tiles(f"W1 {j}", w1, n, UT)
                        feature_tiles(f"W3 {j}", w3, n, UT)
                        if 1 <= j <= 8:
                            ada("next", j - 1)
                            ada("nextx", j - 1)
                        j += 1
                    release(2)
                for p in range(2):
                    keys = [f"W2 {p} {tt}" for tt in range(NT)]
                    tiles = [open_tile(k) for k in keys]
                    for kg in range(3):
                        w = panel(l)
                        if kg == 0 and p == 0:
                            pe.wait_ge(dve_done, DV.at("W3 10 drained"))
                        kn = min(KD, FFT - KD * kg)
                        for tt in range(NT):
                            for i in range(kn):
                                k = KD * kg + i
                                mm(tiles[tt][:, :PW], GT[:, k, tt * P:tt * P + P], w[:, i, :], start=(k == 0),
                                   stop=(k == FFT - 1), done=keys[tt] if k == FFT - 1 else None)
                        release()
                pe.wait_ge(pe_done, PE.count)
                pe.sem_inc(panels_free, st["free"] + LAYER_SLOTS - len(LAYER_PANELS))
                st["free"] = 0
                phase_over()

            uses = [len([i for i in range(len(LAYER_PANELS)) if i % RING == s]) for s in range(RING)]

            def tail_panel():
                n = st["tail"]
                st["tail"] += 1
                pe.wait_ge(panel_in[n % RING], 16 * (DEPTH * uses[n % RING] + n // RING + 1))
                return ring[:, n % RING]

            def normed_transposes(tag, place, tiles_):
                dg = norm_places(place)[1]
                per = 4 // tiles_
                for j in range(KD // per):
                    key = f"{tag} {j}"
                    ps = open_tile(key)
                    for e in range(per):
                        for tt in range(tiles_):
                            pe.wait_ge(dve_done, DV.at(f"dg {tag} {tt}"))
                            ft = per * j + e
                            mm(ps[:, (e * tiles_ + tt) * P:(e * tiles_ + tt + 1) * P], X[:, tt, ft * P:ft * P + P], dg[:, tt, :],
                               done=key if e * tiles_ + tt == 3 else None)

            def out_projection(tag, x, tiles_):
                for p in range(2):
                    w = tail_panel()
                    for tt in range(tiles_):
                        token_tile(f"{tag} {p} {tt}", w, tt, x)
                    release()

            def mlp(tag, tiles_, extra):
                wide = tiles_ * P
                j = 0
                per = 4 // tiles_
                for p in range(MLP // PW):
                    w = tail_panel()
                    for n in range(4 // per):
                        key = f"{tag} in {j}"
                        ps = open_tile(key)
                        for e in range(per):
                            for i in range(KD):
                                c = (n * per + e) * P
                                mm(ps[:, e * wide:e * wide + wide], w[:, i, c:c + P], UT2[:, i, :wide], start=(i == 0),
                                   stop=(i == KD - 1), done=key if e == per - 1 and i == KD - 1 else None)
                        extra(j)
                        j += 1
                    release()
                hid = GT2 if tiles_ == 4 else GT2n
                for p in range(2):
                    keys = [f"{tag} out {p} {tt}" for tt in range(tiles_)]
                    tiles = [open_tile(k) for k in keys]
                    for kg in range(MT // KD):
                        w = tail_panel()
                        if p == 0 and kg == 0:
                            pe.wait_ge(act_done, AC.at(f"{tag} hidden"))
                        for tt in range(tiles_):
                            for i in range(KD):
                                k = KD * kg + i
                                mm(tiles[tt][:, :PW], hid[:, k, tt * P:tt * P + P], w[:, i, :], start=(k == 0),
                                   stop=(k == MT - 1), done=keys[tt] if k == MT - 1 else None)
                        release()

            def adas(q, tags):
                for tag in tags:
                    ada(tag, q)

            pe.wait_ge(phase_go, DEPTH + 1)
            pe.sem_inc(phase_seen, 1)
            PE.start("attn")
            st.update(n=0, tail=0, acc=0)
            normed_transposes("X", "attn", 4)
            for j in range(8):
                drained(f"X {j}")
            pe.wait_ge(par2_in, 32)
            j = 0
            for p in range(2):
                w = tail_panel()
                for i in range(4):
                    key = f"Q {j}"
                    ps = open_tile(key)
                    for k in range(KD):
                        mm(ps[:, :], w[:, k, i * P:i * P + P], UT2[:, k, :], start=(k == 0), stop=(k == KD - 1), done=key if k == KD - 1 else None)
                    if j:
                        adas(8 + j - 1, ("ada", "adax"))
                    j += 1
                release()
            w = tail_panel()
            for j in range(2):
                key = f"K {j}"
                ps = open_tile(key)
                for k in range(KD):
                    mm(ps[:, :], w[:, k, j * P:j * P + P], UT2[:, k, :], start=(k == 0), stop=(k == KD - 1), done=key if k == KD - 1 else None)
            adas(15, ("ada", "adax"))
            for j in range(2):
                key = f"V {j}"
                ps = open_tile(key)
                for e in range(2):
                    tt = 2 * j + e
                    for k in range(KD):
                        mm(ps[:, e * T:e * T + T], UT2[:, k, tt * P:tt * P + P], w[:, k, T:2 * T], start=(k == 0), stop=(k == KD - 1),
                           done=key if e and k == KD - 1 else None)
            release()
            for m in range(5):
                key = f"R {m}"
                x = QT[:, 2 * m:2 * m + 2, :T] if m < 4 else KT[:, :, :T]
                for e in range(2):
                    pe.wait_ge(act_done, AC.at((f"Q {2 * m + e}" if m < 4 else f"K {e}") + " drained"))
                ps = open_tile(key)
                mm(ps[:, :], rot, x, done=key)
            for i in range(HEADS + 1):
                if i < HEADS:
                    if i == 0:
                        pe.wait_ge(dve_done, DV.at("rope 4"))
                    jj, b, ii = i // 8, (i % 8) // 4, i % 4
                    q, k = QT[HD * b:HD * b + HD, 4 * jj + ii, :], KT[HD * b:HD * b + HD, jj, :]
                    for tt in range(2):
                        key = f"SL {i} {tt}"
                        ps = open_tile(key)
                        mm(ps[:, :], q[:, tt * P:tt * P + P], k, done=key)
                    key = f"SX {i}"
                    ps = open_tile(key)
                    for tt in range(2):
                        mm(ps[:, tt * T:tt * T + T], q[:, T + tt * P:T + tt * P + P], k[:, T:2 * T], done=key if tt else None)
                    if i in ADA_HEADS:
                        adas(16 + ADA_HEADS.index(i), ("ada", "adax"))
                if i:
                    n = i - 1
                    pe.wait_ge(dve_done, DV.at(f"hprobs {n}"))
                    lat = SCA[n % 2][:, :1024].rearrange("p (t s) -> p t s", t=2)
                    con = SCA[n % 2][:, 1024:].rearrange("p (t s) -> p t s", t=2)
                    for g in range(3):
                        key = f"TP {n} {g}"
                        ps = open_tile(key)
                        for j in range(4):
                            kt, tt = j // 2, j % 2
                            x = lat[:, tt, (2 * g + kt) * P:(2 * g + kt + 1) * P] if g < 2 else con[:, tt, kt * P:kt * P + P]
                            mm(ps[:, j * P:j * P + P], x, ident, t=True, done=key if j == 3 else None)
                    key = f"AV {n}"
                    ps = open_tile(key)
                    if n == 0:
                        for j in range(2):
                            pe.wait_ge(act_done, AC.at(f"V {j} drained"))
                    p0 = HD * (n % 2)
                    kv = n // (HEADS // KV)
                    for j in range(6):
                        pe.wait_ge(act_done, AC.at(f"TP {n} {j // 2} drained"))
                        kt, c0 = (j, 0) if j < 4 else (j - 2, T)
                        mm(ps[p0:p0 + HD, c0:c0 + T], VT[:, kt, kv * HD:kv * HD + HD], PTA[:, n % 2, j, :], start=(j in (0, 4)),
                           stop=(j in (3, 5)), done=key if j == 5 else None)
            for n in range(HEADS):
                pe.wait_ge(act_done, AC.at(f"AV {n} drained"))
            out_projection("mix", UT2, 4)
            normed_transposes("Y", "attn", 4)
            for j in range(8):
                drained(f"Y {j}")

            def attn_extra(j):
                if j >= 3 and j % 2 and (j - 3) // 2 < 12:
                    n = (j - 3) // 2
                    adas((ADA_TAIL + ADA_NEXT)[n], ("ada", "adax") if n < 4 else ("next", "nextx"))

            mlp("mlp", 4, attn_extra)
            phase_over()

            pe.wait_ge(phase_go, DEPTH + 2)
            pe.sem_inc(phase_seen, 1)
            PE.start("gla")
            st.update(n=0, acc=0)
            normed_transposes("X", "gla", 4)
            for j in range(8):
                drained(f"X {j}")
            seq = list(ADA_LATER)
            for p in range(2):
                w = tail_panel()
                for n in range(2):
                    feature_tiles(f"GG {2 * p + n}", w, n, UT2[:, :, :T])
                    if 2 * p + n:
                        for _ in range(2):
                            adas(seq.pop(0), ("ada",))
                release()
            for p in range(2):
                w = tail_panel()
                for tt in range(4):
                    token_tile(f"GV {p} {tt}", w, tt, UT2)
                    for _ in range(2 if p == 0 and tt < 2 else 1):
                        if seq:
                            adas(seq.pop(0), ("ada",))
                release()
            while seq:
                adas(seq.pop(0), ("ada",))
            pe.wait_ge(par2_in, 48)
            ps = open_tile("DN")
            for k in range(KD):
                mm(ps[:64, :], w_down[:, k, :], UT2[:, k, :], start=(k == 0), stop=(k == KD - 1), done="DN" if k == KD - 1 else None)
            wk, wq = tail_panel(), tail_panel()

            def gk(h):
                key = f"GK {h}"
                ps = open_tile(key)
                for k in range(KD):
                    mm(ps[:, :], wk[:, k, h * P:h * P + P], UT2[:, k, :], start=(k == 0), stop=(k == KD - 1), done=key if k == KD - 1 else None)
                key = f"GQ {h}"
                ps = open_tile(key)
                for k in range(KD):
                    mm(ps[:, :T], wq[:, k, h * P:h * P + P], UT2[:, k, :T], start=(k == 0), stop=(k == KD - 1), done=key if k == KD - 1 else None)

            def gz_(h):
                for d in range(2):
                    key = f"Z {h} {d}"
                    ps = open_tile(key)
                    if h == 0 and d == 0:
                        pe.wait_ge(act_done, AC.at("DN drained"))
                    mm(ps[:, :], w_up[32 * d:32 * d + 16, h * P:h * P + P], gDT[32 * d:32 * d + 16, :], done=key)

            gz_(0)
            gk(0)
            for h in range(G_HEADS):
                if h + 1 < G_HEADS:
                    gk(h + 1)
                pe.wait_ge(dve_done, DV.at(f"gprep {h}"))
                for b in range(2):
                    key = f"KK {h} {b}"
                    ps = open_tile(key)
                    for j in range(4 if b == 0 else 2):
                        x = gKE[:, j // 2, T + (j % 2) * P:T + (j % 2) * P + P] if b == 0 else gKL[:, j, :]
                        mm(ps[:, j * P:j * P + P], x, ident, t=True, done=key if j == (3 if b == 0 else 1) else None)
                for tt in range(NT):
                    key = f"GA {h} {tt}"
                    ps = open_tile(key)
                    for d in range(2):
                        for e, k in enumerate((gKI, gKE)):
                            j = 2 * d + e
                            mm(ps[:, j * P:j * P + P], k[:, d, tt * P:tt * P + P], gQD[:, d, tt * P:tt * P + P], done=key if j == 3 else None)
                for b in range(2):
                    pe.wait_ge(act_done, AC.at(f"KK {h} {b} drained"))
                if h == 0:
                    for p in range(2):
                        for tt in range(4):
                            pe.wait_ge(act_done, AC.at(f"GV {p} {tt} drained"))
                hv = slice(h * G_DV, (h + 1) * G_DV)
                ps = open_tile(f"GS0 {h}")
                for d in range(2):
                    for c in range(2):
                        mm(ps[:, d * T:d * T + T], gKK[:, 2 * d + c, :], gV[:, 2 + c, hv], start=(c == 0), stop=(c == 1),
                           done=f"GS0 {h}" if d and c else None)
                ps = open_tile(f"GS1 {h}")
                for d in range(2):
                    mm(ps[:, d * T:d * T + T], gKK[:, 4 + d, :], gV[:, d, hv], done=f"GS1 {h}" if d else None)
                ps = open_tile(f"GO {h}")
                for tt in range(NT):
                    pe.wait_ge(dve_done, DV.at(f"gat {h} {tt}"))
                    mm(ps[:, tt * T:tt * T + T], gAT[:, tt, :], gV[:, tt, hv], start=True, stop=False)
                    pe.wait_ge(act_done, AC.at(f"GS0 {h} drained"))
                    pe.wait_ge(dve_done, DV.at(f"GS1 {h} drained"))
                    for d in range(2):
                        mm(ps[:, tt * T:tt * T + T], gQL[:, d, tt * P:tt * P + P], gS[:, tt if d == 0 else 1 - tt, d, :], start=False,
                           stop=(d == 1), done=f"GO {h}" if tt and d else None)
                if h + 1 < G_HEADS:
                    gz_(h + 1)
                pe.wait_ge(dve_done, DV.at(f"ghn {h}"))
                ps = open_tile(f"GH {h}")
                for j in range(4):
                    mm(ps[:, j * P:j * P + P], gHN[:, j % 2, (j // 2) * P:(j // 2) * P + P], ident, t=True, done=f"GH {h}" if j == 3 else None)
            release(2)
            pe.wait_ge(dve_done, DV.at("GH 3 drained"))
            out_projection("mix", gOT, 2)
            normed_transposes("Y", "gla", 2)
            for j in range(4):
                drained(f"Y {j}")
            mlp("mlp", 2, lambda j: None)
            phase_over()

        @block.scalar
        def _(act):
            def func(out, x, f, **kw):
                return nc.scalar.activation(out, x, f, **kw)

            def drain(key, out, f=ACT.Copy):
                return nc.scalar.activation(out, tile(key)[:, :out.free_size()], f)

            def modulated(tag, i):
                act.wait_ge(pe_done, PE.at(f"{tag} {i} full"))
                ps = tile(f"{tag} {i}")
                for j in range(2):
                    ft = 2 * i + j
                    func(UT[:, ft, :], ps[:, j * T:j * T + T], ACT.Identity, scale=colA[:, ft:ft + 1],
                        bias=colB[:, ft:ft + 1]).then_inc(
                        act_done, AC.drained(f"{tag} {i}" if j else None))

            def ada(tag, q):
                key = f"{tag} {q}"
                act.wait_ge(pe_done, PE.at(key + " full"))
                ps = tile(key)
                sec, part = q // 4, q % 4
                x = tag in ("nextx", "adax")
                if sec in (2, 5):
                    row = grow[:, x if Progress.phase == "attn" else sec // 5, part * HP:part * HP + HP]
                    func(row, ps[:, :HP], ACT.Copy).then_inc(act_done, AC.drained(key))
                else:
                    func((adacx if x else adac)[:, sec, 2 * part:2 * part + 2], ps[:, 0:2 * P:P], ACT.Copy).then_inc(
                        act_done, AC.drained(key))

            def rstds(name):
                act.wait_ge(dve_done, DV.at(name + " moments"))
                func(rstd[:, :], mv[:, :, 1], ACT.Ln, bias=LN_EPS).then_inc(act_done, AC.step())
                act.wait_ge(act_done, AC.count)
                func(rstd[:, :], rstd[:, :], ACT.Exp, scale=-0.5).then_inc(act_done, AC.step(name + " rstd"))

            def act_mini(h, s):
                if s == 0:
                    act.wait_ge(dve_done, DV.at(f"negmax {h}"))
                    for j in range(4):
                        func(Am[:, j // 2, j % 2, :], Am[:, j // 2, j % 2, :], ACT.Exp, bias=small[:, 1, j:j + 1]).then_inc(
                            act_done, AC.step())
                    func(small[:, 3, :], small[:, 2, :], ACT.Exp, scale=-1.0).then_inc(act_done, AC.step(f"exp {h}"))
                elif s == 1:
                    if h:
                        act.wait_ge(pe_done, PE.at(f"HV {h - 1} full"))
                    act.wait_ge(pe_done, PE.at(f"PTT {h} full"))
                    drain(f"PTT {h}", PTm[:, :, :].rearrange("p a b -> p (a b)")).then_inc(
                        act_done, AC.drained(f"PTT {h}"))
                elif s == 2:
                    rstds(f"head {h}")

            def phase_over():
                act.wait_ge(act_done, AC.count)
                act.sem_inc(phase_end, 1)

            AC.start("start")
            act.wait_ge(x_in, 32)
            func(colA[:, :], csil[:, 0, :], ACT.Sigmoid).then_inc(act_done, AC.step())
            func(adac[:, 0:2, :].rearrange("p a b -> p (a b)"), csil[:, 3:5, :].rearrange("p a b -> p (a b)"), ACT.Sigmoid).then_inc(
                act_done, AC.step("sigmoid c"))
            rstds("x")
            for q in ADA_NEXT:
                ada("ada", q)
            phase_over()

            with act.Fori(0, DEPTH) as l:
                act.wait_ge(phase_go, l + 1)
                act.sem_inc(phase_seen, 1)
                AC.start("layer")
                act.dma_start(area(par, NPAR), a["params"][bass.ds(l, 1)].rearrange("a p n -> (a p) n")).then_inc(params_in, 16)
                act.dma_start(rows[:, :, :].rearrange("p a b -> p (a b)"),
                              a["ln_prev"][bass.ds(l, 1)].rearrange("a b -> (a b)").partition_broadcast(P)).then_inc(rows1_in, 16)
                act.wait_ge(dve_done, DV.at("cols T"))
                for i in (0, 2):
                    modulated("T", i)
                act.wait_ge(dve_done, DV.at("gates abs"))
                func(gw[:, 1, :], gw[:, 0, :], ACT.Exp, scale=-1.0).then_inc(act_done, AC.step())
                act.wait_ge(act_done, AC.count)
                func(gw[:, 2, :], gw[:, 1, :], ACT.Ln, bias=1.0).then_inc(act_done, AC.step("softplus"))
                for n in range(8):
                    act.wait_ge(dve_done, DV.at(f"conv {n}"))
                    func(QK[:, 2 * n:2 * n + 2, :].rearrange("p a b -> p (a b)"),
                        cbuf[:, 2 * (n % 2):2 * (n % 2) + 2, :].rearrange("p a b -> p (a b)"), ACT.Silu).then_inc(
                        act_done, AC.step(f"silu {n}"))
                for nj in range(8):
                    if nj < 4:
                        act.wait_ge(pe_done, PE.at(f"O {nj} full"))
                        drain(f"O {nj}", SIG[:, 2 * nj:2 * nj + 2, :].rearrange("p a b -> p (a b)"), ACT.Sigmoid).then_inc(
                            act_done, AC.drained(f"O {nj}"))
                    else:
                        n = nj - 4
                        if n == 0:
                            act.wait_ge(dve_done, DV.at("h T"))
                        act.wait_ge(pe_done, PE.at(f"VM {n} full"))
                        drain(f"VM {n}", VM[:, n % 2, PW * (n // 2):PW * (n // 2) + PW]).then_inc(
                            act_done, AC.drained(f"VM {n}"))
                    if nj:
                        for q in ADA_LATER[2 * nj - 2:2 * nj]:
                            ada("ada", q)
                for q in ADA_LATER[14:]:
                    ada("ada", q)
                for n in range(12):
                    x, m = (AQ, n) if n < 6 else (AK, n - 6)
                    act.wait_ge(pe_done, PE.at(f"AQK {n} full"))
                    drain(f"AQK {n}", x[:, 2 * m:2 * m + 2, :].rearrange("p a b -> p (a b)")).then_inc(
                        act_done, AC.drained(f"AQK {n}"))
                    for h, s in minis(n):
                        act_mini(h, s)
                for n in range(6):
                    act.wait_ge(pe_done, PE.at(f"VA {n} full"))
                    drain(f"VA {n}", VA[:, n % 2, PW * (n // 2):PW * (n // 2) + PW]).then_inc(
                        act_done, AC.drained(f"VA {n}"))
                act.dma_start(rows[:, :, :].rearrange("p a b -> p (a b)"),
                              a["ln_mid"][bass.ds(l, 1)].rearrange("a b -> (a b)").partition_broadcast(P)).then_inc(rows2_in, 16)
                for i in range(SLOTS + 1):
                    if i < SLOTS:
                        act.wait_ge(dve_done, DV.at(f"slot negmax {i}"))
                        for tt in range(NT):
                            func(SC[i % 2][:, tt, :], SC[i % 2][:, tt, :], ACT.Exp, scale=A_DIM ** -0.5,
                                bias=att[:, i % 2, 1, tt:tt + 1], accum_out=att[:, i % 2, 2, tt:tt + 1]).then_inc(
                                act_done, AC.step(f"slot exp {i}" if tt else None))
                    if i:
                        n = i - 1
                        if n >= 2:
                            act.wait_ge(pe_done, PE.at(f"AV {n - 2} full"))
                        for g in range(NPAT):
                            act.wait_ge(pe_done, PE.at(f"PT {n} {g} full"))
                            drain(f"PT {n} {g}", PT[:, n % 2, 2 * g:2 * g + 2, :].rearrange("p a b -> p (a b)")).then_inc(
                                act_done, AC.drained(f"PT {n} {g}"))
                        act.wait_ge(pe_done, PE.at(f"AV {n} full"))
                        ps = tile(f"AV {n}")
                        p0 = A_DIM * (n % 2)
                        func(OAT[p0:p0 + A_DIM, n // 2, :], ps[p0:p0 + A_DIM, :T], ACT.Copy).then_inc(
                            act_done, AC.drained(f"AV {n}"))
                for p in range(2):
                    for b, name in enumerate(("GA", "GB")):
                        for n in range(2):
                            j = 2 * p + n
                            if p:
                                act.wait_ge(dve_done, DV.at(f"mix {j - 2}"))
                            act.wait_ge(pe_done, PE.at(f"{name} {j} full"))
                            drain(f"{name} {j}", sg[:, 2 * n + b, :], ACT.Sigmoid).then_inc(
                                act_done, AC.drained(f"{name} {j}"))
                rstds("ln1")
                act.wait_ge(dve_done, DV.at("cols U"))
                for i in (0, 2):
                    modulated("U", i)
                for j in range(FFT // 2):
                    if j >= 4:
                        act.wait_ge(dve_done, DV.at(f"W3 {j - 4} drained"))
                    act.wait_ge(pe_done, PE.at(f"W1 {j} full"))
                    drain(f"W1 {j}", sg[:, j % 4, :], ACT.Silu).then_inc(act_done, AC.drained(f"W1 {j}"))
                    if 1 <= j <= 8:
                        ada("next", j - 1)
                        ada("nextx", j - 1)
                rstds("ln2")
                phase_over()

            def flat(x):
                return x.rearrange("p a b -> p (a b)")

            def squares(tag, at, tt, half, x):
                act.wait_ge(pe_done, PE.at(f"{tag} {half} {tt} full"))
                ps = tile(f"{tag} {half} {tt}")
                act.wait_ge(act_done, AC.count)
                func(norm_places(at)[3][:, :PW], ps[:, :PW], ACT.Square, accum_out=ssq[:, half, tt:tt + 1]).then_inc(
                    act_done, AC.step())

            def post_rstd(tag, at, tiles_):
                for tt in range(tiles_):
                    squares(tag, at, tt, 0, None)
                for tt in range(tiles_):
                    squares(tag, at, tt, 1, None)
                    act.wait_ge(act_done, AC.count)
                    func(aux1[:, tt:tt + 1], ssq[:, 0, tt:tt + 1], ACT.Identity, scale=1.0 / D, bias=RMS_EPS).then_inc(
                        act_done, AC.step())
                    act.wait_ge(act_done, AC.count)
                    func(rst[:, tt:tt + 1], ssq[:, 1, tt:tt + 1], ACT.Ln, scale=1.0 / D, bias=aux1[:, tt:tt + 1]).then_inc(
                        act_done, AC.step())
                    act.wait_ge(act_done, AC.count)
                    func(rst[:, tt:tt + 1], rst[:, tt:tt + 1], ACT.Exp, scale=-0.5).then_inc(
                        act_done, AC.step(f"{tag} rstd {tt}"))

            def pre_rstd(tag, at, tiles_, after):
                for tt in range(tiles_):
                    if after:
                        act.wait_ge(dve_done, DV.at(f"{after} {tt}"))
                    act.wait_ge(act_done, AC.count)
                    func(norm_places(at)[3], X[:, tt, :], ACT.Square, accum_out=ssq[:, 0, tt:tt + 1]).then_inc(
                        act_done, AC.step())
                    act.wait_ge(act_done, AC.count)
                    func(rst[:, tt:tt + 1], ssq[:, 0, tt:tt + 1], ACT.Ln, scale=1.0 / D, bias=RMS_EPS).then_inc(
                        act_done, AC.step())
                    act.wait_ge(act_done, AC.count)
                    func(rst[:, tt:tt + 1], rst[:, tt:tt + 1], ACT.Exp, scale=-0.5).then_inc(
                        act_done, AC.step(f"{tag} pre {tt}"))

            def modulated2(tag, j, tiles_, sec):
                act.wait_ge(pe_done, PE.at(f"{tag} {j} full"))
                ps = tile(f"{tag} {j}")
                if tiles_ == 4:
                    for x, sh in ((0, adac), (1, adacx)):
                        func(UT2[:, j, x * T:x * T + T], ps[:, x * T:x * T + T], ACT.Identity, scale=colX[:, x, j:j + 1],
                            bias=sh[:, sec, j:j + 1]).then_inc(
                            act_done, AC.drained(f"{tag} {j}" if x else None))
                else:
                    for e in range(2):
                        ft = 2 * j + e
                        func(UT2[:, ft, :T], ps[:, e * T:e * T + T], ACT.Identity, scale=colX[:, 0, ft:ft + 1],
                            bias=adac[:, sec, ft:ft + 1]).then_inc(
                            act_done, AC.drained(f"{tag} {j}" if e else None))

            def mlp(tag, tiles_, extra):
                hid = GT2 if tiles_ == 4 else GT2n
                per = 4 // tiles_
                for j in range(MT // per):
                    act.wait_ge(pe_done, PE.at(f"{tag} in {j} full"))
                    ps = tile(f"{tag} in {j}")
                    x = hid[:, per * j:per * j + per, :].rearrange("p a b -> p (a b)")
                    func(x, ps[:, :], ACT.Relu).then_inc(act_done, AC.drained(f"{tag} in {j}"))
                    act.wait_ge(act_done, AC.count)
                    func(x, x, ACT.Square).then_inc(act_done, AC.step(f"{tag} hidden" if j == MT // per - 1 else None))
                    extra(j)

            def adas(q, tags):
                for tag in tags:
                    ada(tag, q)

            act.wait_ge(phase_go, DEPTH + 1)
            act.sem_inc(phase_seen, 1)
            AC.start("attn")
            act.dma_start(flat(rows[:, :, :]), a["ln_prev"][DEPTH].partition_broadcast(P)).then_inc(rows2_in, 16)
            act.dma_start(X[:, 2:4, :], a["ctx"].rearrange("(t p) n -> p t n", p=P)).then_inc(ctx_in, 16)
            act.dma_start(area(M["CST"] + 2 * P, NC2), a["consts_attn"]).then_inc(par2_in, 16)
            act.dma_start(area(par2, NP2), a["params2"]).then_inc(par2_in, 16)
            gp = norm_places("attn")[0]
            act.dma_start(gp, a["post"][0].partition_broadcast(P)).then_inc(rows1_in, 16)
            act.wait_ge(ctx_in, 16)
            for tt in (2, 3, 0, 1):
                if tt < 2:
                    act.wait_ge(dve_done, DV.at("x 1"))
                act.wait_ge(act_done, AC.count)
                func(norm_places("attn")[3], X[:, tt, :], ACT.Square, accum_out=ssq[:, 0, tt:tt + 1]).then_inc(
                    act_done, AC.step())
                act.wait_ge(act_done, AC.count)
                func(rst[:, tt:tt + 1], ssq[:, 0, tt:tt + 1], ACT.Ln, scale=1.0 / D, bias=RMS_EPS).then_inc(act_done, AC.step())
                act.wait_ge(act_done, AC.count)
                func(rst[:, tt:tt + 1], rst[:, tt:tt + 1], ACT.Exp, scale=-0.5).then_inc(act_done, AC.step(f"X pre {tt}"))
            act.wait_ge(dve_done, DV.at("colX X"))
            for j in range(0, 8, 2):
                modulated2("X", j, 4, 0)
            for j in range(8):
                act.wait_ge(pe_done, PE.at(f"Q {j} full"))
                drain(f"Q {j}", QT[:, j, :]).then_inc(act_done, AC.drained(f"Q {j}"))
                if j:
                    adas(8 + j - 1, ("ada", "adax"))
            for j in range(2):
                act.wait_ge(pe_done, PE.at(f"K {j} full"))
                drain(f"K {j}", KT[:, j, :]).then_inc(act_done, AC.drained(f"K {j}"))
            adas(15, ("ada", "adax"))
            for j in range(2):
                act.wait_ge(pe_done, PE.at(f"V {j} full"))
                drain(f"V {j}", flat(VT[:, 2 * j:2 * j + 2, :])).then_inc(act_done, AC.drained(f"V {j}"))
            for i in range(HEADS + 1):
                if i < HEADS:
                    act.wait_ge(dve_done, DV.at(f"hmax {i}"))
                    lat = SCA[i % 2][:, :1024].rearrange("p (t s) -> p t s", t=2)
                    con = SCA[i % 2][:, 1024:].rearrange("p (t s) -> p t s", t=2)
                    st_ = hst[:, i % 2]
                    for tt in range(2):
                        func(lat[:, tt, :], lat[:, tt, :], ACT.Exp, scale=HD ** -0.5, bias=st_[:, 1, tt:tt + 1],
                            accum_out=st_[:, 2, tt:tt + 1]).then_inc(
                            act_done, AC.step())
                    act.wait_ge(pe_done, PE.at(f"SX {i} full"))
                    ps = tile(f"SX {i}")
                    for tt in range(2):
                        func(con[:, tt, :], ps[:, tt * T:tt * T + T], ACT.Exp, scale=HD ** -0.5,
                            bias=st_[:, 1, 2 + tt:3 + tt], accum_out=st_[:, 2, 2 + tt:3 + tt]).then_inc(
                            act_done, AC.drained(f"SX {i}" if tt else None))
                    func(st_[:, 3, :], st_[:, 1, :], ACT.Exp, bias=sinks[:, i:i + 1]).then_inc(act_done, AC.step(f"hexp {i}"))
                    if i in ADA_HEADS:
                        adas(16 + ADA_HEADS.index(i), ("ada", "adax"))
                if i:
                    n = i - 1
                    if n >= 2:
                        act.wait_ge(pe_done, PE.at(f"AV {n - 2} full"))
                    for g in range(3):
                        act.wait_ge(pe_done, PE.at(f"TP {n} {g} full"))
                        drain(f"TP {n} {g}", flat(PTA[:, n % 2, 2 * g:2 * g + 2, :])).then_inc(
                            act_done, AC.drained(f"TP {n} {g}"))
                    act.wait_ge(pe_done, PE.at(f"AV {n} full"))
                    ps = tile(f"AV {n}")
                    p0 = HD * (n % 2)
                    func(UT2[p0:p0 + HD, n // 2, :], ps[p0:p0 + HD, :], ACT.Copy).then_inc(
                        act_done, AC.drained(f"AV {n}"))
            post_rstd("mix", "attn", 4)
            pre_rstd("Y", "attn", 4, "mix x")
            act.wait_ge(dve_done, DV.at("colX Y"))
            for j in range(0, 8, 2):
                modulated2("Y", j, 4, 3)

            def attn_extra(j):
                if j >= 3 and j % 2 and (j - 3) // 2 < 12:
                    n = (j - 3) // 2
                    adas((ADA_TAIL + ADA_NEXT)[n], ("ada", "adax") if n < 4 else ("next", "nextx"))

            mlp("mlp", 4, attn_extra)
            act.dma_start(norm_places("attn mlp")[0], a["post"][1].partition_broadcast(P)).then_inc(rows2_in, 16)
            post_rstd("mlp out", "attn mlp", 4)
            pre_rstd("next", "attn mlp", 4, "mlp out x")
            phase_over()

            act.wait_ge(phase_go, DEPTH + 2)
            act.sem_inc(phase_seen, 1)
            AC.start("gla")
            act.dma_start(area(M["CST"] + 2 * P, 4 * P + 2 * T), a["consts_gla"]).then_inc(par2_in, 16)
            act.wait_ge(dve_done, DV.at("colX X"))
            for j in range(0, 8, 2):
                modulated2("X", j, 4, 0)
            seq = list(ADA_LATER)
            for j in range(4):
                act.wait_ge(pe_done, PE.at(f"GG {j} full"))
                drain(f"GG {j}", flat(gOT[:, 2 * j:2 * j + 2, :]), ACT.Silu).then_inc(act_done, AC.drained(f"GG {j}"))
                if j:
                    for _ in range(2):
                        adas(seq.pop(0), ("ada",))
            for p in range(2):
                for tt in range(4):
                    act.wait_ge(pe_done, PE.at(f"GV {p} {tt} full"))
                    drain(f"GV {p} {tt}", gV[:, tt, PW * p:PW * p + PW]).then_inc(act_done, AC.drained(f"GV {p} {tt}"))
                    for _ in range(2 if p == 0 and tt < 2 else 1):
                        if seq:
                            adas(seq.pop(0), ("ada",))
            while seq:
                adas(seq.pop(0), ("ada",))
            act.wait_ge(pe_done, PE.at("DN full"))
            ps = tile("DN")
            func(gDT[:64, :], ps[:64, :], ACT.Copy).then_inc(act_done, AC.drained("DN"))

            def gprep(h, d):
                if d or h:
                    act.wait_ge(dve_done, DV.at(f"gargs {h if d else h - 1} {0 if d else 1}"))
                act.wait_ge(pe_done, PE.at(f"Z {h} {d} full"))
                ps = tile(f"Z {h} {d}")
                func(gZ, ps[:, :], ACT.Identity, bias=g_bias[:, d, h:h + 1]).then_inc(
                    act_done, AC.drained(f"Z {h} {d}"))
                act.wait_ge(dve_done, DV.at(f"gabs {h} {d}"))
                func(gL, gL, ACT.Exp, scale=-1.0).then_inc(act_done, AC.step())
                act.wait_ge(act_done, AC.count)
                func(gL, gL, ACT.Ln, bias=1.0).then_inc(act_done, AC.step(f"gln {h} {d}"))
                act.wait_ge(dve_done, DV.at(f"gargs {h} {d}"))
                b = gC[:, :T] if d == 0 else gQD[:, 1, :]
                func(gKI[:, d, :], b, ACT.Exp, scale=-1.0 / G_TAU).then_inc(act_done, AC.step())
                act.wait_ge(act_done, AC.count)
                func(gQD[:, d, :], b, ACT.Exp, scale=1.0 / G_TAU).then_inc(act_done, AC.step())
                func(gKE[:, d, :], gKE[:, d, :], ACT.Exp, scale=(-1.0 if d == 0 else 1.0) / G_TAU).then_inc(act_done, AC.step())
                func(gdec[:, d, 0:4], gC[:, G_CHUNK - 1:T:G_CHUNK], ACT.Exp, scale=1.0 / G_TAU).then_inc(
                    act_done, AC.step(f"gexp {h} {d}"))

            def gkq(h):
                act.wait_ge(pe_done, PE.at(f"GK {h} full"))
                drain(f"GK {h}", gKT[:, h, :]).then_inc(act_done, AC.drained(f"GK {h}"))
                act.wait_ge(pe_done, PE.at(f"GQ {h} full"))
                ps = tile(f"GQ {h}")
                func(gQT[:, h, :], ps[:, :T], ACT.Copy, scale=G_DK ** -0.5).then_inc(act_done, AC.drained(f"GQ {h}"))

            gprep(0, 0)
            gprep(0, 1)
            gkq(0)
            for h in range(G_HEADS):
                if h + 1 < G_HEADS:
                    gkq(h + 1)
                for b in range(2):
                    n = 4 if b == 0 else 2
                    act.wait_ge(pe_done, PE.at(f"KK {h} {b} full"))
                    drain(f"KK {h} {b}", flat(gKK[:, 4 * b:4 * b + n, :])).then_inc(act_done, AC.drained(f"KK {h} {b}"))
                act.wait_ge(pe_done, PE.at(f"GS0 {h} full"))
                drain(f"GS0 {h}", flat(gS[:, 0, :, :])).then_inc(act_done, AC.drained(f"GS0 {h}"))
                act.wait_ge(pe_done, PE.at(f"GO {h} full"))
                ps = tile(f"GO {h}")
                for tt in range(NT):
                    act.wait_ge(act_done, AC.count)
                    func(gHN[:, tt, :], ps[:, tt * T:tt * T + T], ACT.Square, accum_out=gst[:, tt:tt + 1]).then_inc(
                        act_done, AC.step())
                act.wait_ge(act_done, AC.count)
                func(gst[:, 2:4], gst[:, 0:2], ACT.Ln, scale=1.0 / G_DV, bias=RMS_EPS).then_inc(act_done, AC.step())
                act.wait_ge(act_done, AC.count)
                func(gst[:, 4:6], gst[:, 2:4], ACT.Exp, scale=-0.5).then_inc(act_done, AC.step(f"grstd {h}"))
                if h + 1 < G_HEADS:
                    gprep(h + 1, 0)
                    gprep(h + 1, 1)
            act.dma_start(norm_places("gla")[0], a["post"][2].partition_broadcast(P)).then_inc(rows1_in, 16)
            post_rstd("mix", "gla", 2)
            pre_rstd("Y", "gla", 2, "mix x")
            act.wait_ge(dve_done, DV.at("colX Y"))
            for j in (0, 2):
                modulated2("Y", j, 2, 3)
            mlp("mlp", 2, lambda j: None)
            act.dma_start(norm_places("gla mlp")[0], a["post"][3].partition_broadcast(P)).then_inc(rows2_in, 16)
            post_rstd("mlp out", "gla mlp", 2)
            phase_over()

        @block.vector
        def _(dve):
            V = nc.vector
            st = {"ada": 0, "acc": 0}

            def tt_(out, x, y, op):
                return V.tensor_tensor(out, x, y, op)

            def ts(out, x, s1, s2, op0, op1=None):
                return V.tensor_scalar(out, x, s1, s2, op0, op1) if op1 is not None else V.tensor_scalar(out, x, s1, None, op0)

            def stt(out, x, s, y, op0, op1, **kw):
                return V.scalar_tensor_tensor(out=out, in0=x, scalar=s, in1=y, op0=op0, op1=op1, **kw)

            def ada(q, n, s, conds):
                dve.wait_ge(ada_in[n % ADA_SLOTS], s)
                w = adaw[:, n % ADA_SLOTS]
                xs = []
                for tag, c in conds:
                    xs.append(acc[:, st["acc"] % ACC_SLOTS, :])
                    if st["acc"] >= ACC_SLOTS:
                        dve.wait_ge(pe_done, PE.at(st[st["acc"] - ACC_SLOTS] + " full"))
                    st[st["acc"]] = f"{tag} {q}"
                    st["acc"] += 1
                for k in range(KD):
                    for x, (tag, c) in zip(xs, conds):
                        stt(x, w[:, k, :], c[:, k:k + 1], w[:, KD, :] if k == 0 else x, ALU.mult, ALU.add).then_inc(
                            dve_done, DV.step(f"{tag} {q} acc" if k == KD - 1 else None))
                    dve.wait_ge(dve_done, DV.count)
                dve.sem_inc(ada_free, 1)

            def columns(tag, sec):
                g = ln_cols[:, 0 if tag == "T" else 2, :]
                b = ln_cols[:, 1 if tag == "T" else 3, :]
                ts(colT[:, :], adac[:, sec + 1, :], 1.0, None, ALU.add).then_inc(dve_done, DV.step())
                dve.wait_ge(dve_done, DV.count)
                tt_(colA[:, :], colT[:, :], g, ALU.mult).then_inc(dve_done, DV.step())
                tt_(colB[:, :], colT[:, :], b, ALU.mult).then_inc(dve_done, DV.step())
                dve.wait_ge(dve_done, DV.count)
                tt_(colB[:, :], colB[:, :], adac[:, sec, :], ALU.add).then_inc(dve_done, DV.step(f"cols {tag}"))

            def modulated(tag, i):
                dve.wait_ge(pe_done, PE.at(f"{tag} {i} full"))
                ps = tile(f"{tag} {i}")
                for j in range(2):
                    ft = 2 * i + j
                    ts(UT[:, ft, :], ps[:, j * T:j * T + T], colA[:, ft:ft + 1], colB[:, ft:ft + 1], ALU.mult, ALU.add).then_inc(
                        dve_done, DV.drained(f"{tag} {i}" if j else None))

            def affine(tag):
                dve.wait_ge(pe_done, PE.at(f"{tag} 3 full"))
                for tt in range(NT):
                    tt_(H[:, tt, :], H[:, tt, :], rows[:, 0, :], ALU.mult).then_inc(dve_done, DV.step())
                dve.wait_ge(dve_done, DV.count)
                for tt in range(NT):
                    tt_(H[:, tt, :], H[:, tt, :], rows[:, 1, :], ALU.add).then_inc(
                        dve_done, DV.step(f"h {tag}" if tt else None))

            def moments(tt):
                for half in range(2):
                    o = 12 * tt + 6 * half
                    V.bn_stats(stats[:, o:o + 6], H[:, tt, PW * half:PW * half + PW]).then_inc(dve_done, DV.step())

            def normalise(name):
                dve.wait_ge(dve_done, DV.count)
                for tt in range(NT):
                    V.bn_aggr(mv[:, tt, :], stats[:, 12 * tt:12 * tt + 12]).then_inc(
                        dve_done, DV.step(name + " moments" if tt else None))
                dve.wait_ge(act_done, AC.at(name + " rstd"))
                dve.wait_ge(dve_done, DV.count)
                for tt in range(NT):
                    ts(H[:, tt, :], H[:, tt, :], mv[:, tt, 0:1], rstd[:, tt:tt + 1], ALU.subtract, ALU.mult).then_inc(
                        dve_done, DV.step(name if tt else None))

            def residual(key, tt, half, g):
                n = 2 * half + tt
                dve.wait_ge(pe_done, PE.at(key + " full"))
                ps = tile(key)
                if n >= 2:
                    dve.wait_ge(dve_done, DV.count)
                tt_(lnt[:, n % 2, :], ps[:, :], grow[:, g, PW * half:PW * half + PW], ALU.mult).then_inc(
                    dve_done, DV.drained(key))
                dve.wait_ge(dve_done, DV.count)
                x = H[:, tt, PW * half:PW * half + PW]
                stt(x, x, ALPHA, lnt[:, n % 2, :], ALU.mult, ALU.add).then_inc(dve_done, DV.step())
                dve.wait_ge(dve_done, DV.count)
                V.bn_stats(stats[:, 12 * tt + 6 * half:12 * tt + 6 * half + 6], x).then_inc(dve_done, DV.step())

            def make_diag(h):
                if h:
                    dve.wait_ge(pe_done, PE.at(f"A {h - 1} full"))
                for j in range(4):
                    ts(diag[:, j, :], ident, aB[:, 0, j // 2, j % 2, h:h + 1], None, ALU.mult).then_inc(
                        dve_done, DV.step(f"diag {h}" if j == 3 else None))

            def dve_mini(h, s):
                if s == 0:
                    dve.wait_ge(pe_done, PE.at(f"A {h} full"))
                    ps = tile(f"A {h}")
                    row = ps[:, :].rearrange("p (d s) -> p d s", d=2).unsqueeze(2).to_broadcast([P, 2, NT, T])
                    tt_(Am[:, :, :, :], row, masks[:, :, :, :], ALU.add).then_inc(dve_done, DV.drained(f"A {h}"))
                    dve.wait_ge(dve_done, DV.count)
                    V.reduce_max(small[:, 0, :].rearrange("p (d t) -> p d t", d=2), Am[:, :, :, :], AX.X).then_inc(
                        dve_done, DV.step())
                    dve.wait_ge(dve_done, DV.count)
                    tt_(small[:, 2, :].rearrange("p (d t) -> p d t", d=2), small[:, 0, :].rearrange("p (d t) -> p d t", d=2),
                        aB[:, 1, :, :, h], ALU.add).then_inc(
                        dve_done, DV.step())
                    ts(small[:, 1, :], small[:, 0, :], -1.0, None, ALU.mult).then_inc(dve_done, DV.step(f"negmax {h}"))
                    if h + 1 < M_HEADS:
                        make_diag(h + 1)
                    dve.wait_ge(pe_done, PE.at(f"S {h} full"))
                    ps = tile(f"S {h}")
                    dve.wait_ge(act_done, AC.at(f"exp {h}"))
                    for j in range(4):
                        stt(Am[:, j // 2, j % 2, :], ps[:, (j % 2) * T:(j % 2) * T + T], M_DIM ** -0.5,
                            Am[:, j // 2, j % 2, :], ALU.mult, ALU.mult, accum_out=small[:, 4, j:j + 1]).then_inc(
                            dve_done, DV.drained(f"S {h}" if j == 3 else None))
                    dve.wait_ge(dve_done, DV.count)
                    stt(small[:, 5, :], small[:, 4, :], -1.0, small[:, 4, :], ALU.mult, ALU.max).then_inc(dve_done, DV.step())
                    dve.wait_ge(dve_done, DV.count)
                    tt_(small[:, 5, :], small[:, 5, :], small[:, 3, :], ALU.max).then_inc(dve_done, DV.step())
                    dve.wait_ge(dve_done, DV.count)
                    V.reciprocal(small[:, 6, :], small[:, 5, :]).then_inc(dve_done, DV.step())
                    dve.wait_ge(dve_done, DV.count)
                    if h:
                        dve.wait_ge(pe_done, PE.at(f"PTT {h - 1} full"))
                    for tt in range(NT):
                        ts(Pm[:, tt, :], Am[:, 0, tt, :], small[:, 6, tt:tt + 1], None, ALU.mult).then_inc(dve_done, DV.step())
                    dve.wait_ge(dve_done, DV.count)
                    for tt in range(NT):
                        stt(Pm[:, tt, :], Am[:, 1, tt, :], small[:, 6, 2 + tt:3 + tt], Pm[:, tt, :], ALU.mult, ALU.add).then_inc(
                            dve_done, DV.step(f"P {h}" if tt else None))
                elif s == 2:
                    dve.wait_ge(pe_done, PE.at(f"HV {h} full"))
                    ps = tile(f"HV {h}")
                    for tt in range(NT):
                        V.bn_stats(stats[:, 6 * tt:6 * tt + 6], ps[:, tt * T:tt * T + T]).then_inc(dve_done, DV.step())
                    dve.wait_ge(dve_done, DV.count)
                    for tt in range(NT):
                        V.bn_aggr(mv[:, tt, :], stats[:, 6 * tt:6 * tt + 6]).then_inc(
                            dve_done, DV.step(f"head {h} moments" if tt else None))
                    dve.wait_ge(act_done, AC.at(f"head {h} rstd"))
                    dve.wait_ge(dve_done, DV.count)
                    for tt in range(NT):
                        ts(hn[:, tt, :], ps[:, tt * T:tt * T + T], mv[:, tt, 0:1], rstd[:, tt:tt + 1], ALU.subtract,
                            ALU.mult).then_inc(
                            dve_done, DV.drained(f"HV {h}" if tt else None))
                    marks[Progress.phase, "dve", f"hn {h}"] = DV.count
                elif s == 3:
                    dve.wait_ge(pe_done, PE.at(f"HT {h} full"))
                    ps = tile(f"HT {h}")
                    dve.wait_ge(act_done, AC.at("O 3 drained"))
                    for ft in range(2):
                        x = SIG[:, 2 * h + ft, :]
                        stt(x, ps[:, ft * T:ft * T + T], gn_w[:, 2 * h + ft:2 * h + ft + 1], x, ALU.mult, ALU.mult).then_inc(
                            dve_done, DV.drained(f"HT {h}" if ft else None))
                    if h == M_HEADS - 1:
                        marks[Progress.phase, "dve", "y_m"] = DV.count

            def phase_over(n):
                dve.wait_ge(dve_done, DV.count)
                dve.wait_ge(phase_end, n)
                dve.sem_inc(phase_seen, 1)
                dve.sem_clear(range(pe_done.num, rows2_in.num + 1))
                dve.sem_inc(phase_go, 1)

            DV.start("start")
            V.memset(adaw[:, :, KD, :], 0.0).then_inc(dve_done, DV.step())
            dve.wait_ge(dve_done, DV.count)
            dve.sem_inc(ada_free, ADA_SLOTS)
            dve.wait_ge(x_in, 32)
            for tt in range(NT):
                moments(tt)
            dve.wait_ge(act_done, AC.at("sigmoid c"))
            tt_(csil[:, 0, :], csil[:, 0, :], colA[:, :], ALU.mult).then_inc(dve_done, DV.step())
            tt_(csil[:, 3:5, :], csil[:, 3:5, :], adac[:, 0:2, :], ALU.mult).then_inc(dve_done, DV.step())
            dve.wait_ge(dve_done, DV.count)
            for j, c in ((1, 0), (2, 3)):
                V.tensor_copy(csil[:, j, :], csil[:, c, :]).then_inc(dve_done, DV.step())
            normalise("x")
            for n, q in enumerate(ADA_NEXT):
                ada(q, n, 32 * (n // ADA_SLOTS + 1), [("ada", csil[:, 0, :])])
            phase_over(2)

            with dve.Fori(0, DEPTH) as l:
                DV.start("layer")
                st.update(ada=0, acc=0)

                def ada_turn(q, conds):
                    n = st["ada"]
                    st["ada"] += 1
                    ada(q, n, l * (24 // ADA_SLOTS * 32) + 32 * ((8 + n) // ADA_SLOTS + 1), conds)

                own = csil[:, bass.ds(l, 1), :].rearrange("p a k -> p (a k)")
                nxt = csil[:, bass.ds(l + 1, 1), :].rearrange("p a k -> p (a k)")
                dve.wait_ge(params_in, 16)
                columns("T", 0)
                for i in (1, 3):
                    if i == 1:
                        dve.wait_ge(dve_done, DV.count)
                    modulated("T", i)
                dve.wait_ge(rows1_in, 16)
                affine("T")
                dve.wait_ge(pe_done, PE.at("G full"))
                ps = tile("G")
                for tt in range(NT):
                    tt_(gz[:, tt, :], ps[:, tt * 16:tt * 16 + 16], bg_row, ALU.add).then_inc(
                        dve_done, DV.drained("G" if tt else None))
                dve.wait_ge(dve_done, DV.count)
                z = gz[:, :, :].rearrange("p a b -> p (a b)")
                stt(gw[:, 0, :], z, -1.0, z, ALU.mult, ALU.max).then_inc(dve_done, DV.step("gates abs"))
                dve.wait_ge(act_done, AC.at("softplus"))
                stt(gw[:, 3, :], z, 0.0, gw[:, 2, :], ALU.min, ALU.subtract).then_inc(dve_done, DV.step("lf"))
                for n in range(8):
                    dve.wait_ge(pe_done, PE.at(f"QK {n} full"))
                    ps = tile(f"QK {n}")
                    if n >= 2:
                        dve.wait_ge(act_done, AC.at(f"silu {n - 2}"))
                    cb = [cbuf[:, 2 * (n % 2) + j, :] for j in range(2)]
                    w = [conv_w[:, 2 * n + j, :] for j in range(2)]
                    for j in range(2):
                        ts(cb[j], ps[:, j * T:j * T + T], w[j][:, 2:3], conv_b[:, 2 * n + j:2 * n + j + 1], ALU.mult,
                            ALU.add).then_inc(
                            dve_done, DV.step())
                    for tap in (0, 1, 3, 4):
                        dve.wait_ge(dve_done, DV.count)
                        d = tap - 2
                        lo, hi = max(0, -d), T - max(0, d)
                        for j in range(2):
                            stt(cb[j][:, lo:hi], ps[:, j * T + lo + d:j * T + hi + d], w[j][:, tap:tap + 1], cb[j][:, lo:hi],
                                ALU.mult, ALU.add).then_inc(
                                dve_done, DV.drained(f"QK {n}" if tap == 4 and j else None))
                    marks[Progress.phase, "dve", f"conv {n}"] = DV.count
                    if n == 1:
                        dve.wait_ge(pe_done, PE.at("CS full"))
                        ps = tile("CS")
                        for d in range(2):
                            cs = ps[:, d * 32:d * 32 + 32].rearrange("p (t g) -> p t g", t=NT)[:, :, 8 * d + 4:8 * d + 8]
                            tt_(aB[:, 0, d, :, :], gz[:, :, 8 * d:8 * d + 4], cs, ALU.subtract).then_inc(dve_done, DV.step())
                            V.tensor_copy(aB[:, 1, d, :, :], cs).then_inc(dve_done, DV.drained("CS" if d else None))
                for q in ADA_LATER:
                    ada_turn(q, [("ada", own)])
                dve.wait_ge(dve_done, DV.count)
                make_diag(0)
                for n in range(12):
                    for h, s in minis(n):
                        dve_mini(h, s)
                for i in range(SLOTS + 1):
                    if i < SLOTS:
                        if i >= 2:
                            dve.wait_ge(pe_done, PE.at(f"PT {i - 2} 2 full"))
                        x = SC[i % 2]
                        for g in range(NPAT):
                            dve.wait_ge(pe_done, PE.at(f"SC {i} {g} full"))
                            ps = tile(f"SC {i} {g}")
                            stt(x[:, :, g * T:g * T + T], dist[:, g, :].rearrange("p (t s) -> p t s", t=NT),
                                float(SLOPES[g, i]) * A_DIM ** 0.5, ps[:, :].rearrange("p (t s) -> p t s", t=NT), ALU.mult, ALU.add).then_inc(
                                dve_done, DV.drained(f"SC {i} {g}"))
                        dve.wait_ge(dve_done, DV.count)
                        V.reduce_max(att[:, i % 2, 0, :], x[:, :, :], AX.X).then_inc(dve_done, DV.step())
                        dve.wait_ge(dve_done, DV.count)
                        ts(att[:, i % 2, 1, :], att[:, i % 2, 0, :], -A_DIM ** -0.5, None, ALU.mult).then_inc(
                            dve_done, DV.step(f"slot negmax {i}"))
                    if i:
                        n = i - 1
                        dve.wait_ge(act_done, AC.at(f"slot exp {n}"))
                        V.reciprocal(att[:, n % 2, 3, :], att[:, n % 2, 2, :]).then_inc(dve_done, DV.step())
                        dve.wait_ge(dve_done, DV.count)
                        for tt in range(NT):
                            ts(SC[n % 2][:, tt, :], SC[n % 2][:, tt, :], att[:, n % 2, 3, tt:tt + 1], None, ALU.mult).then_inc(
                                dve_done, DV.step(f"probs {n}" if tt else None))
                for p in range(2):
                    for n in range(2):
                        j = 2 * p + n
                        dve.wait_ge(pe_done, PE.at(f"WA {j} full"))
                        ps = tile(f"WA {j}")
                        dve.wait_ge(act_done, AC.at(f"GA {j} drained"))
                        tt_(MIX[:, 2 * j:2 * j + 2, :].rearrange("p a b -> p (a b)"), ps[:, :], sg[:, 2 * n, :], ALU.mult).then_inc(
                            dve_done, DV.drained(f"WA {j}"))
                    for n in range(2):
                        j = 2 * p + n
                        dve.wait_ge(pe_done, PE.at(f"WB {j} full"))
                        ps = tile(f"WB {j}")
                        dve.wait_ge(act_done, AC.at(f"GB {j} drained"))
                        x = MIX[:, 2 * j:2 * j + 2, :].rearrange("p a b -> p (a b)")
                        tt_(sg[:, 2 * n + 1, :], ps[:, :], sg[:, 2 * n + 1, :], ALU.mult).then_inc(
                            dve_done, DV.drained(f"WB {j}"))
                        dve.wait_ge(dve_done, DV.count)
                        tt_(x, x, sg[:, 2 * n + 1, :], ALU.add).then_inc(dve_done, DV.step(f"mix {j}"))
                for half in range(2):
                    for tt in range(NT):
                        residual(f"WO {half} {tt}", tt, half, 0)
                normalise("ln1")
                columns("U", 3)
                dve.wait_ge(dve_done, DV.count)
                for i in (1, 3):
                    modulated("U", i)
                dve.wait_ge(rows2_in, 16)
                affine("U")
                for j in range(FFT // 2):
                    dve.wait_ge(pe_done, PE.at(f"W3 {j} full"))
                    ps = tile(f"W3 {j}")
                    dve.wait_ge(act_done, AC.at(f"W1 {j} drained"))
                    tt_(GT[:, 2 * j:2 * j + 2, :].rearrange("p a b -> p (a b)"), ps[:, :], sg[:, j % 4, :], ALU.mult).then_inc(
                        dve_done, DV.drained(f"W3 {j}"))
                    if j < 8:
                        ada_turn(j, [("next", nxt), ("nextx", csil[:, 4, :])])
                for half in range(2):
                    for tt in range(NT):
                        residual(f"W2 {half} {tt}", tt, half, 1)
                normalise("ln2")
                phase_over(l * 2 + 4)

            tail = {"ada": 0}

            def tail_ada(q, conds):
                n = tail["ada"]
                tail["ada"] += 1
                ada(q, n, 32 * ((8 + 24 * DEPTH + n) // ADA_SLOTS + 1), conds)

            def gain_columns(tag, which, sec, both):
                for x in range(2 if both else 1):
                    ts(colX[:, x, :], (adacx if x else adac)[:, sec + 1, :], 1.0, None, ALU.add).then_inc(dve_done, DV.step())
                dve.wait_ge(dve_done, DV.count)
                for x in range(2 if both else 1):
                    tt_(colX[:, x, :], colX[:, x, :], gains[:, which, :], ALU.mult).then_inc(
                        dve_done, DV.step(f"colX {tag}" if x == both else None))
                dve.wait_ge(dve_done, DV.count)

            def diagonals(tag, at, tiles_):
                for tt in range(tiles_):
                    dve.wait_ge(act_done, AC.at(f"{tag} pre {tt}"))
                    ts(norm_places(at)[1][:, tt, :], ident, rst[:, tt:tt + 1], None, ALU.mult).then_inc(
                        dve_done, DV.step(f"dg {tag} {tt}"))

            def modulated2(tag, j, tiles_, sec):
                dve.wait_ge(pe_done, PE.at(f"{tag} {j} full"))
                ps = tile(f"{tag} {j}")
                if tiles_ == 4:
                    for x, sh in ((0, adac), (1, adacx)):
                        ts(UT2[:, j, x * T:x * T + T], ps[:, x * T:x * T + T], colX[:, x, j:j + 1], sh[:, sec, j:j + 1],
                            ALU.mult, ALU.add).then_inc(
                            dve_done, DV.drained(f"{tag} {j}" if x else None))
                else:
                    for e in range(2):
                        ft = 2 * j + e
                        ts(UT2[:, ft, :T], ps[:, e * T:e * T + T], colX[:, 0, ft:ft + 1], adac[:, sec, ft:ft + 1], ALU.mult,
                            ALU.add).then_inc(
                            dve_done, DV.drained(f"{tag} {j}" if e else None))

            def post(tag, at, tiles_, rows_used, rows_sem, n):
                gp, _, tmp, _ = norm_places(at)
                dve.wait_ge(rows_sem, n)
                dve.wait_ge(dve_done, DV.count)
                for x in rows_used:
                    tt_(grow[:, x, :], grow[:, x, :], gp, ALU.mult).then_inc(dve_done, DV.step())
                for tt in range(tiles_):
                    dve.wait_ge(act_done, AC.at(f"{tag} rstd {tt}"))
                    for half in range(2):
                        key = f"{tag} {half} {tt}"
                        dve.wait_ge(pe_done, PE.at(key + " full"))
                        ps = tile(key)
                        dve.wait_ge(dve_done, DV.count)
                        stt(tmp[:, half, :], ps[:, :], rst[:, tt:tt + 1],
                            grow[:, rows_used[tt // 2], PW * half:PW * half + PW], ALU.mult, ALU.mult).then_inc(
                            dve_done, DV.drained(key))
                    dve.wait_ge(dve_done, DV.count)
                    x = X[:, tt, :]
                    tt_(x, x, tmp.rearrange("p a b -> p (a b)"), ALU.add).then_inc(dve_done, DV.step(f"{tag} x {tt}"))

            wide = {"ada": csil[:, 2, :], "adax": csil[:, 4, :], "next": csil[:, 3, :], "nextx": csil[:, 4, :]}
            DV.start("attn")
            st.update(acc=0)
            dve.wait_ge(rows2_in, 16)
            for tt in range(NT):
                tt_(H[:, tt, :], H[:, tt, :], rows[:, 0, :], ALU.mult).then_inc(dve_done, DV.step())
            dve.wait_ge(dve_done, DV.count)
            for tt in range(NT):
                tt_(H[:, tt, :], H[:, tt, :], rows[:, 1, :], ALU.add).then_inc(dve_done, DV.step(f"x {tt}"))
            dve.wait_ge(par2_in, 32)
            gain_columns("X", 0, 0, True)
            ts(sink8, sinks, HD ** 0.5, None, ALU.mult).then_inc(dve_done, DV.step())
            dve.wait_ge(act_done, AC.at("X pre 1"))
            for tt in range(4):
                ts(norm_places("attn")[1][:, tt, :], ident, rst[:, tt:tt + 1], None, ALU.mult).then_inc(
                    dve_done, DV.step(f"dg X {tt}"))
            for j in range(1, 8, 2):
                modulated2("X", j, 4, 0)
            for j in range(8):
                tail_ada(8 + j, [(t, wide[t]) for t in ("ada", "adax")])
            for m in range(5):
                dve.wait_ge(pe_done, PE.at(f"R {m} full"))
                ps = tile(f"R {m}")
                x = QT[:, 2 * m:2 * m + 2, :T] if m < 4 else KT[:, :, :T]
                y = ps[:, :].rearrange("p (a b) -> p a b", a=2)
                tmp = SCA[m % 2][:, :2 * T].rearrange("p (a b) -> p a b", a=2)
                dve.wait_ge(dve_done, DV.count)
                tt_(tmp, y, sinT.unsqueeze(1).to_broadcast([P, 2, T]), ALU.mult).then_inc(
                    dve_done, DV.drained(f"R {m}"))
                tt_(x, x, cosT.unsqueeze(1).to_broadcast([P, 2, T]), ALU.mult).then_inc(dve_done, DV.step())
                dve.wait_ge(dve_done, DV.count)
                tt_(x, x, tmp, ALU.add).then_inc(dve_done, DV.step(f"rope {m}"))
            for i in range(HEADS + 1):
                if i < HEADS:
                    if i >= 2:
                        dve.wait_ge(pe_done, PE.at(f"TP {i - 2} 2 full"))
                    elif i == 0:
                        dve.wait_ge(dve_done, DV.count)
                    lat = SCA[i % 2][:, :1024].rearrange("p (t s) -> p t s", t=2)
                    st_ = hst[:, i % 2]
                    for tt in range(2):
                        dve.wait_ge(pe_done, PE.at(f"SL {i} {tt} full"))
                        ps = tile(f"SL {i} {tt}")
                        tt_(lat[:, tt, :], ps[:, :], band[:, tt, :], ALU.add).then_inc(
                            dve_done, DV.drained(f"SL {i} {tt}"))
                    dve.wait_ge(pe_done, PE.at(f"SX {i} full"))
                    ps = tile(f"SX {i}")
                    V.reduce_max(st_[:, 0, 2:4], ps[:, :].rearrange("p (t s) -> p t s", t=2), AX.X).then_inc(
                        dve_done, DV.step())
                    dve.wait_ge(dve_done, DV.count)
                    V.reduce_max(st_[:, 0, 0:2], lat, AX.X).then_inc(dve_done, DV.step())
                    dve.wait_ge(dve_done, DV.count)
                    ts(st_[:, 1, :], st_[:, 0, :], sink8[:, i:i + 1], -HD ** -0.5, ALU.max, ALU.mult).then_inc(
                        dve_done, DV.step(f"hmax {i}"))
                    if i in ADA_HEADS:
                        tail_ada(16 + ADA_HEADS.index(i), [(t, wide[t]) for t in ("ada", "adax")])
                if i:
                    n = i - 1
                    lat = SCA[n % 2][:, :1024].rearrange("p (t s) -> p t s", t=2)
                    con = SCA[n % 2][:, 1024:].rearrange("p (t s) -> p t s", t=2)
                    st_ = hst[:, n % 2]
                    dve.wait_ge(act_done, AC.at(f"hexp {n}"))
                    tt_(st_[:, 4, :], st_[:, 2, :], st_[:, 3, :], ALU.add).then_inc(dve_done, DV.step())
                    dve.wait_ge(dve_done, DV.count)
                    V.reciprocal(st_[:, 5, :], st_[:, 4, :]).then_inc(dve_done, DV.step())
                    dve.wait_ge(dve_done, DV.count)
                    for tt in range(2):
                        ts(lat[:, tt, :], lat[:, tt, :], st_[:, 5, tt:tt + 1], None, ALU.mult).then_inc(dve_done, DV.step())
                    for tt in range(2):
                        ts(con[:, tt, :], con[:, tt, :], st_[:, 5, 2 + tt:3 + tt], None, ALU.mult).then_inc(
                            dve_done, DV.step(f"hprobs {n}" if tt else None))
            dve.wait_ge(act_done, AC.at("adax 11 drained"))
            post("mix", "attn", 4, (0, 1), rows1_in, 16)
            dve.wait_ge(act_done, AC.at("adax 19 drained"))
            gain_columns("Y", 1, 3, True)
            diagonals("Y", "attn", 4)
            for j in range(1, 8, 2):
                modulated2("Y", j, 4, 3)
            for n, q in enumerate(ADA_TAIL + ADA_NEXT):
                tail_ada(q, [(t, wide[t]) for t in (("ada", "adax") if n < 4 else ("next", "nextx"))])
            dve.wait_ge(act_done, AC.at("adax 23 drained"))
            post("mlp out", "attn mlp", 4, (0, 1), rows2_in, 32)
            for tt in range(4):
                dve.wait_ge(act_done, AC.at(f"next pre {tt}"))
                ts(norm_places("gla")[1][:, tt, :], ident, rst[:, tt:tt + 1], None, ALU.mult).then_inc(dve_done, DV.step())
            phase_over(2 * DEPTH + 4)

            DV.start("gla")
            st.update(acc=0)
            V.memset(gst[:, 8:9], 0.0).then_inc(dve_done, DV.step("dg X 0"))
            for tt in range(1, 4):
                marks[Progress.phase, "dve", f"dg X {tt}"] = 1
            gain_columns("X", 2, 0, True)
            for j in range(1, 8, 2):
                modulated2("X", j, 4, 0)
            for q in ADA_LATER:
                tail_ada(q, [("ada", csil[:, 3, :])])
            dve.wait_ge(par2_in, 48)

            def chunked(x):
                return x.rearrange("p (c s) -> p c s", s=G_CHUNK)

            def gprep(h, d):
                dve.wait_ge(act_done, AC.at(f"Z {h} {d} drained"))
                dve.wait_ge(dve_done, DV.count)
                stt(gL, gZ, -1.0, gZ, ALU.mult, ALU.max).then_inc(dve_done, DV.step(f"gabs {h} {d}"))
                dve.wait_ge(act_done, AC.at(f"gln {h} {d}"))
                dve.wait_ge(dve_done, DV.count)
                stt(gZ, gZ, 0.0, gL, ALU.min, ALU.subtract).then_inc(dve_done, DV.step())
                dve.wait_ge(dve_done, DV.count)
                V.tensor_tensor_scan(gC, keep, gZ, 0.0, ALU.mult, ALU.add).then_inc(dve_done, DV.step())
                dve.wait_ge(dve_done, DV.count)
                if h:
                    dve.wait_ge(pe_done, PE.at(f"GO {h - 1} full"))
                ends = gC[:, G_CHUNK - 1:T:G_CHUNK].unsqueeze(2).to_broadcast([P, T // G_CHUNK, G_CHUNK])
                if d == 0:
                    tt_(chunked(gKE[:, 0, :T]), chunked(gC[:, :T]), ends, ALU.subtract).then_inc(dve_done, DV.step())
                    ts(gKE[:, 0, T:], gC[:, T:], gC[:, 2 * T - 1:2 * T], None, ALU.subtract).then_inc(
                        dve_done, DV.step(f"gargs {h} {d}"))
                else:
                    tt_(gKE[:, 1, :], gC, gZ, ALU.subtract).then_inc(dve_done, DV.step())
                    dve.wait_ge(dve_done, DV.count)
                    tt_(chunked(gQD[:, 1, :]), ends, chunked(gKE[:, 1, :T]), ALU.subtract).then_inc(
                        dve_done, DV.step(f"gargs {h} {d}"))
                dve.wait_ge(act_done, AC.at(f"gexp {h} {d}"))
                if d == 1:
                    dve.wait_ge(act_done, AC.at(f"GQ {h} drained"))
                    dve.wait_ge(act_done, AC.at(f"GK {h} drained"))
                    for e in range(2):
                        tt_(gQD[:, e, :], gQD[:, e, :], gQT[:, h, :], ALU.mult).then_inc(dve_done, DV.step())
                        tt_(gKI[:, e, :], gKI[:, e, :], gKT[:, h, :T], ALU.mult).then_inc(dve_done, DV.step())
                        tt_(gKE[:, e, :], gKE[:, e, :], gKT[:, h, :], ALU.mult).then_inc(dve_done, DV.step())
                    dve.wait_ge(dve_done, DV.count)
                    for e in range(2):
                        q = gQD[:, e, :].rearrange("p (t c s) -> p t c s", t=2, c=2)
                        ql = gQL[:, e, :].rearrange("p (t c s) -> p t c s", t=2, c=2)
                        V.tensor_copy(ql[:, :, e, :], q[:, :, e, :]).then_inc(dve_done, DV.step())
                        dec = gdec[:, e, e:4:2].unsqueeze(2).to_broadcast([P, 2, G_CHUNK])
                        tt_(ql[:, :, 1 - e, :], q[:, :, 1 - e, :], dec, ALU.mult).then_inc(dve_done, DV.step())
                        k = gKE[:, e, e * P:e * P + P].rearrange("p (c s) -> p c s", c=2)
                        kl = gKL[:, e, :].rearrange("p (c s) -> p c s", c=2)
                        V.tensor_copy(kl[:, 1 - e, :], k[:, 1 - e, :]).then_inc(dve_done, DV.step())
                        other = gdec[:, e, 1:2] if e == 0 else gdec[:, e, 2:3]
                        ts(kl[:, e, :], k[:, e, :], other, None, ALU.mult).then_inc(dve_done, DV.step())
                        tt_(gdec[:, e, 4:5], gdec[:, e, 2 * e:2 * e + 1], gdec[:, e, 2 * e + 1:2 * e + 2], ALU.mult).then_inc(
                            dve_done, DV.step(f"gprep {h}" if e else None))

            gprep(0, 0)
            gprep(0, 1)
            for h in range(G_HEADS):
                for tt in range(NT):
                    dve.wait_ge(pe_done, PE.at(f"GA {h} {tt} full"))
                    ps = tile(f"GA {h} {tt}")
                    if tt == 0:
                        dve.wait_ge(dve_done, DV.count)
                    tmp = (gZ, gL)[tt]
                    tt_(tmp, ps[:, :], gmask, ALU.mult).then_inc(dve_done, DV.drained(f"GA {h} {tt}"))
                    dve.wait_ge(dve_done, DV.count)
                    tt_(tmp[:, :T], tmp[:, :T], tmp[:, T:], ALU.add).then_inc(dve_done, DV.step())
                    dve.wait_ge(dve_done, DV.count)
                    tt_(gAT[:, tt, :], tmp[:, :P], tmp[:, P:T], ALU.add).then_inc(dve_done, DV.step(f"gat {h} {tt}"))
                dve.wait_ge(pe_done, PE.at(f"GS1 {h} full"))
                ps = tile(f"GS1 {h}")
                dve.wait_ge(act_done, AC.at(f"GS0 {h} drained"))
                for d in range(2):
                    stt(gS[:, 1, d, :], gS[:, 0, d, :], gdec[:, d, 4:5], ps[:, d * T:d * T + T], ALU.mult, ALU.add).then_inc(
                        dve_done, DV.drained(f"GS1 {h}" if d else None))
                dve.wait_ge(pe_done, PE.at(f"GO {h} full"))
                ps = tile(f"GO {h}")
                dve.wait_ge(act_done, AC.at(f"grstd {h}"))
                for tt in range(NT):
                    ts(gHN[:, tt, :], ps[:, tt * T:tt * T + T], gst[:, 4 + tt:5 + tt], None, ALU.mult).then_inc(
                        dve_done, DV.drained(f"GO {h}" if tt else None))
                marks[Progress.phase, "dve", f"ghn {h}"] = DV.count
                if h + 1 < G_HEADS:
                    gprep(h + 1, 0)
                    gprep(h + 1, 1)
                dve.wait_ge(pe_done, PE.at(f"GH {h} full"))
                ps = tile(f"GH {h}")
                for ft in range(2):
                    x = gOT[:, 2 * h + ft, :]
                    stt(x, ps[:, ft * T:ft * T + T], g_norm[:, ft:ft + 1], x, ALU.mult, ALU.mult).then_inc(
                        dve_done, DV.drained(f"GH {h}" if ft else None))
            dve.wait_ge(act_done, AC.at("ada 11 drained"))
            post("mix", "gla", 2, (0,), rows1_in, 16)
            dve.wait_ge(act_done, AC.at("ada 19 drained"))
            gain_columns("Y", 3, 3, False)
            diagonals("Y", "gla", 2)
            for j in (1, 3):
                modulated2("Y", j, 2, 3)
            dve.wait_ge(act_done, AC.at("ada 23 drained"))
            post("mlp out", "gla mlp", 2, (1,), rows2_in, 16)
            phase_over(2 * DEPTH + 6)

        @block.sync
        def _(sp):
            sp.dma_start(H[:, :, :], a["x"].rearrange("(t p) n -> p t n", p=P)).then_inc(x_in, 16)
            sp.dma_start(csil[:, :, :], a["conds"]).then_inc(x_in, 16)
            sp.dma_start(cst, a["consts"]).then_inc(cst_in, 16)
            with sp.Fori(0, DEPTH) as l:
                for n, (w, k0, k, c0, cols) in enumerate(LAYER_PANELS):
                    sp.wait_ge(panels_free, l * LAYER_SLOTS + n + 1)
                    src = a[w][bass.ds(l, 1), k0 * P:(k0 + k) * P, c0:c0 + cols].rearrange("a (k p) n -> p (a k) n", p=P)
                    sp.dma_start(ring[:, n % RING, :k, :cols], src).then_inc(panel_in[n % RING], 16)
            for n, (l, w, k0, k, c0, cols) in enumerate(TAIL_PANELS):
                sp.wait_ge(panels_free, DEPTH * LAYER_SLOTS + n + 1)
                src = a[w][l, k0 * P:(k0 + k) * P, c0:c0 + cols].rearrange("(k p) n -> p k n", p=P)
                sp.dma_start(ring[:, n % RING, :k, :cols], src).then_inc(panel_in[n % RING], 16)
            sp.wait_ge(phase_go, DEPTH + 3)
            sp.dma_start(out.rearrange("(t p) n -> p t n", p=P), X[:, 0:2, :]).then_inc(out_done, 16)
            sp.wait_ge(out_done, 16)

        @block.gpsimd
        def _(pool):
            def half_panel(job, q, n, free):
                pool.wait_ge(ada_free, free)
                src = a["w_ada"][job, :, q * HP:q * HP + HP]
                pool.dma_start(adaw[:, n % ADA_SLOTS, :KD, :], src.rearrange("a (k p) n -> p (a k) n", p=P)).then_inc(ada_in[n % ADA_SLOTS], 16)
                pool.dma_start(adaw[0:1, n % ADA_SLOTS, KD, :], a["b_ada"][job, q * HP:q * HP + HP]).then_inc(ada_in[n % ADA_SLOTS], 16)

            for n, q in enumerate(ADA_NEXT):
                half_panel(bass.ds(0, 1), q, n, n + 1)
            with pool.Fori(0, DEPTH) as l:
                for n, q in enumerate(ADA_LATER + ADA_NEXT):
                    half_panel(bass.ds(l if n < 16 else l + 1, 1), q, n, l * 24 + 8 + n + 1)
            first = 8 + 24 * DEPTH
            for n, (job, q) in enumerate([(2, q) for q in ADA_LATER] + [(3, q) for q in ADA_NEXT + ADA_LATER]):
                half_panel(bass.ds(job, 1), q, first + n, first + n + 1)


def host_layout(inputs):
    def tiles(v):
        v = np.asarray(v)
        return np.ascontiguousarray(np.moveaxis(v.reshape(*v.shape[:-1], -1, P), -1, -2))

    f = {k: np.asarray(v) for k, v in inputs.items()}
    w_in = f["w_in"]
    one, zero = np.ones(D, np.float32), np.zeros(D, np.float32)
    params, prev = [], [(one, zero)]
    for l in range(DEPTH):
        prev.append((f["ln2_g"][l], f["ln2_b"][l]))
    for l in range(DEPTH):
        params.append(np.concatenate([
            np.moveaxis(tiles(f["conv_w"][l]), 0, -1).reshape(P, -1),
            tiles(f["conv_b"][l]), tiles(f["gn_w"][l]),
            np.broadcast_to(f["b_gates"][l], (P, 16)),
            np.moveaxis(w_in[l][:, COL_GATE:COL_A].reshape(KD, P, 16), 0, 1).reshape(P, -1),
            tiles(prev[l][0]), tiles(prev[l][1]), tiles(f["ln1_g"][l]), tiles(f["ln1_b"][l])], axis=1))
    c, c2, cc = (tiles(v.reshape(D)) for v in (f["c"], f["c_2"], f["c_ctx_2"]))
    down = np.zeros((KD, P, 64), np.float32)
    up = np.zeros((P, 512), np.float32)
    for d in range(2):
        down[:, :, 32 * d:32 * d + 16] = f["gla_w_gate_down_2"][0, d].reshape(KD, P, 16)
        up[32 * d:32 * d + 16] = f["gla_w_gate_up_2"][0, d]
    params2 = np.concatenate([
        *[tiles(f[n][l]) for l in range(DEPTH) for n in ("g_pre_mix_2", "g_pre_mlp_2")],
        np.broadcast_to(f["attn_sink_2"][0], (P, HEADS)), tiles(f["gla_g_norm_2"][0]),
        *[tiles(f["gla_gate_bias_2"][0, d]) for d in range(2)],
        np.moveaxis(down, 0, 1).reshape(P, -1), up], axis=1)
    consts_attn, consts_gla = second_constants()
    qkv = f["attn_w_qkv_2"]
    pairs = qkv[:, :, :D].reshape(1, D, 2, 2, 4, HD).transpose(0, 1, 2, 4, 3, 5).reshape(1, D, D)
    w_qkv = np.concatenate([pairs, qkv[:, :, D:]], axis=2)
    return {
        "ctx": f["ctx_2"][0], "params2": params2, "consts_attn": consts_attn, "consts_gla": consts_gla,
        "post": np.stack([f[n][l] for l in range(DEPTH) for n in ("g_post_mix_2", "g_post_mlp_2")]),
        "w_qkv": w_qkv, "w_o": f["attn_w_o_2"], "w_gla": f["gla_w_in_2"], "w_gla_o": f["gla_w_o_2"],
        "w_mlp_in": f["w_mlp_in_2"], "w_mlp_out": f["w_mlp_out_2"],
        "x": f["x"][0], "consts": first_constants(), "params": np.stack(params),
        "conds": np.stack([c, c, c2, c2, cc], axis=1),
        "ln_prev": np.stack([np.concatenate(p) for p in prev]),
        "ln_mid": np.stack([np.concatenate([f["ln1_g"][l], f["ln1_b"][l]]) for l in range(DEPTH)]),
        "w_ada": np.concatenate([f["w_ada"], f["w_mod_2"]]), "b_ada": np.concatenate([f["b_ada"], f["b_mod_2"]]),
        **{n: f[n] for n in ("w_in", "w_a", "w_b", "w_out", "w1", "w3", "w2")},
    }


def kernel(**inputs):
    import concourse.bacc as bacc
    from concourse.bass_utils import run_bass_kernel_spmd

    arrays = {k: np.ascontiguousarray(v) for k, v in host_layout(inputs).items()}
    marks = {}
    for _ in range(2):
        nc = bacc.Bacc("TRN2", target_bir_lowering=False, num_devices=1)
        a = {k: nc.dram_tensor(f"in_{k}", v.shape, F32, kind="ExternalInput").ap() for k, v in arrays.items()}
        out = nc.dram_tensor("out", (T, D), F32, kind="ExternalOutput").ap()
        program(nc, a, out, marks)
    r = run_bass_kernel_spmd(nc, [{f"in_{k}": v for k, v in arrays.items()}], core_ids=[0])
    return r.results[0]["out"].reshape(1, T, D)
```
